# Optimizing a Trainium2 kernel written in Bass

```python
import jax, jax.numpy as jnp
from jax import lax
import numpy as np

D_MODEL = 1024
BATCH = 1
SEQ = 512
DEPTH = 1
DEC_BATCH = 8
DEC_SEQ = 8
PAST_LEN = 4096
PAGE_SIZE = 128

BRANCH_W = 512
CHUNK = 128
GM_GROUPS = 8
GM_HD = BRANCH_W // GM_GROUPS
RW_HEADS = 8
RW_HD = BRANCH_W // RW_HEADS
RW_W_LORA = 64
RW_A_LORA = 64
RW_G_LORA = 128
RW_COLS = 3 * BRANCH_W + RW_W_LORA + RW_A_LORA + RW_G_LORA
XA_HEADS = 4
XA_HD = BRANCH_W // XA_HEADS
N_MEM = 256
N_BRANCH = 3
IN_COLS = 2 * BRANCH_W + RW_COLS + BRANCH_W + N_BRANCH * D_MODEL
IN_SPLITS = (BRANCH_W, 2 * BRANCH_W, 2 * BRANCH_W + RW_COLS, 3 * BRANCH_W + RW_COLS)
RW_SPLITS = (BRANCH_W, 2 * BRANCH_W, 3 * BRANCH_W, 3 * BRANCH_W + RW_W_LORA,
             3 * BRANCH_W + RW_W_LORA + RW_A_LORA)
N_GROUPS = 4
EXP_PER_GROUP = 8
EXP_TOPK = 2
EXP_FF = 512
RMS_EPS = 1e-6
LN_EPS = 1e-5
GN_EPS = 64e-5

kernel_name = "hybrid_gmlp_rwkv7_memxattn_hiermoe_step"

def rmsnorm(x, g):
    xf = x.astype(jnp.float32)
    y = xf * lax.rsqrt(jnp.mean(xf * xf, axis=-1, keepdims=True) + RMS_EPS)
    return (y * g.astype(jnp.float32)).astype(x.dtype)

def gmlp_branch(pu, pv, ln_g, ln_b, ws, bs):
    b_, t_, _ = pu.shape
    u = jax.nn.gelu(pu)
    vf = jax.nn.gelu(pv).astype(jnp.float32)
    mu = jnp.mean(vf, axis=-1, keepdims=True)
    var = jnp.mean(jnp.square(vf - mu), axis=-1, keepdims=True)
    vn = ((vf - mu) * lax.rsqrt(var + LN_EPS) * ln_g + ln_b).astype(pu.dtype)
    n_chunks = -(-t_ // CHUNK)
    tp = n_chunks * CHUNK
    vp = jnp.pad(vn, ((0, 0), (0, tp - t_), (0, 0))).reshape(b_, n_chunks, CHUNK, GM_GROUPS, GM_HD)
    w_causal = jnp.tril(ws)
    s = jnp.einsum('gts,bcsgd->bctgd', w_causal, vp) + bs.T[None, None, :, :, None]
    s = s.reshape(b_, tp, BRANCH_W)[:, :t_]
    return u * s, vn

def rwkv_branch(p, prev, s0, mu, w0, w2, a0, a2, g2, k_k, k_a, r_k, lnx_g, lnx_b):
    f32 = jnp.float32
    b_, t_, _ = p.shape
    shifted = jnp.concatenate([prev[:, None, :].astype(p.dtype), p[:, :-1]], axis=1)
    xs = p + (shifted - p) * mu
    r, k, v, wd, ad, gd = jnp.split(xs, RW_SPLITS, axis=-1)
    w_log = -jax.nn.softplus(-(w0 + jnp.tanh(wd) @ w2).astype(f32)) - 0.5
    decay = jnp.exp(-jnp.exp(w_log))
    a = jax.nn.sigmoid((a0 + ad @ a2).astype(f32))
    g = jax.nn.sigmoid(gd) @ g2

    def heads(z):
        return z.reshape(b_, t_, RW_HEADS, RW_HD)

    kf = k.astype(f32)
    kk = heads(kf * k_k)
    kk = kk * lax.rsqrt(jnp.maximum(jnp.sum(kk * kk, axis=-1, keepdims=True), 1e-24))
    kf = kf * (1.0 + (a - 1.0) * k_a)
    rh, kh, vh, wh, ah = heads(r.astype(f32)), heads(kf), heads(v.astype(f32)), heads(decay), heads(a)
    a_vec = -kk
    b_vec = kk * ah

    def step(S, inp):
        r_t, k_t, v_t, w_t, a_t, b_t = inp
        sa = jnp.einsum('bhij,bhj->bhi', S, a_t)
        S = S * w_t[:, :, None, :] + sa[..., None] * b_t[:, :, None, :] + v_t[..., None] * k_t[:, :, None, :]
        y = jnp.einsum('bhij,bhj->bhi', S, r_t)
        return S, y

    def tm(z):
        return jnp.moveaxis(z, 1, 0)

    s_fin, y = lax.scan(step, s0.astype(f32), (tm(rh), tm(kh), tm(vh), tm(wh), tm(a_vec), tm(b_vec)))
    y = jnp.moveaxis(y, 0, 1)
    ym = jnp.mean(y, axis=-1, keepdims=True)
    yv = jnp.mean(jnp.square(y - ym), axis=-1, keepdims=True)
    y = ((y - ym) * lax.rsqrt(yv + GN_EPS)).reshape(b_, t_, BRANCH_W) * lnx_g + lnx_b
    bonus = jnp.sum(rh * kh * r_k, axis=-1, keepdims=True) * vh
    y = (y + bonus.reshape(b_, t_, BRANCH_W)) * g.astype(f32)
    return y.astype(p.dtype), s_fin.astype(p.dtype), p[:, -1]

def mem_attend(q, mem_k, mem_v):
    b_, t_, _ = q.shape
    qh = q.reshape(b_, t_, XA_HEADS, XA_HD)
    s = jnp.einsum('bthd,bmhd->bhtm', qh, mem_k).astype(jnp.float32) * (XA_HD ** -0.5)
    pr = jax.nn.softmax(s, axis=-1).astype(q.dtype)
    o = jnp.einsum('bhtm,bmhd->bthd', pr, mem_v)
    return o.reshape(b_, t_, BRANCH_W)

def hier_moe(x, rg_w, rg_b, re_w, re_b, e_wg, e_wu, e_wd):
    f32 = jnp.float32
    b_, t_, d = x.shape
    xt = x.reshape(-1, d)
    pg = jax.nn.softmax((xt @ rg_w + rg_b).astype(f32), axis=-1)
    g_sel = jnp.argmax(pg, axis=-1)
    pg_top = jnp.max(pg, axis=-1)
    oh_g = jax.nn.one_hot(g_sel, N_GROUPS, dtype=f32)
    le = (jnp.einsum('nd,gde->nge', xt, re_w) + re_b).astype(f32)
    le_sel = jnp.einsum('nge,ng->ne', le, oh_g)
    pe = jax.nn.softmax(le_sel, axis=-1)
    top_v, top_i = lax.top_k(pe, EXP_TOPK)
    top_v = top_v / jnp.sum(top_v, axis=-1, keepdims=True)
    w_exp = jnp.sum(jax.nn.one_hot(top_i, EXP_PER_GROUP, dtype=f32) * top_v[..., None], axis=1)
    comb = (pg_top[:, None, None] * oh_g[:, :, None] * w_exp[:, None, :]).astype(x.dtype)
    out = jnp.zeros_like(xt)
    for gi in range(N_GROUPS):
        h = jax.nn.silu(jnp.einsum('nd,edf->nef', xt, e_wg[gi])) * jnp.einsum('nd,edf->nef', xt, e_wu[gi])
        out = out + jnp.einsum('nef,efd->nd', h * comb[:, gi, :, None], e_wd[gi])
    return out.reshape(b_, t_, d)

def decoder_layer(x, mem_k, mem_v, s0, prev, lw):
    (norm1_g, w_in, gate_b, gm_ln_g, gm_ln_b, gm_ws, gm_bs,
     rw_mu, rw_w0, rw_w2, rw_a0, rw_a2, rw_g2, rw_k_k, rw_k_a, rw_r_k, rw_lnx_g, rw_lnx_b,
     w_branch, w_out, norm2_g, rg_w, rg_b, re_w, re_b, e_wg, e_wu, e_wd) = lw
    b_, t_, _ = x.shape
    xn = rmsnorm(x, norm1_g)
    proj = xn @ w_in
    pu, pv, prw, pq, pgate = jnp.split(proj, IN_SPLITS, axis=-1)
    o_gm, v_rows = gmlp_branch(pu, pv, gm_ln_g, gm_ln_b, gm_ws, gm_bs)
    o_rw, s_new, prev_new = rwkv_branch(prw, prev, s0, rw_mu, rw_w0, rw_w2, rw_a0, rw_a2, rw_g2,
                                        rw_k_k, rw_k_a, rw_r_k, rw_lnx_g, rw_lnx_b)
    o_xa = mem_attend(pq, mem_k, mem_v)
    branches = jnp.stack([o_gm, o_rw, o_xa], axis=2)
    up = jnp.einsum('btnw,nwd->btnd', branches, w_branch)
    gates = jax.nn.sigmoid((pgate + gate_b).astype(jnp.float32)).reshape(b_, t_, N_BRANCH, D_MODEL)
    merged = jnp.sum(gates.astype(x.dtype) * up, axis=2)
    h = x + merged @ w_out
    h = h + hier_moe(rmsnorm(h, norm2_g), rg_w, rg_b, re_w, re_b, e_wg, e_wu, e_wd)
    return h, v_rows, s_new, prev_new

def setup_inputs(seed: int = 0) -> dict:
    key = jax.random.key(seed)
    ks = iter(jax.random.split(key, 48))
    L = DEPTH

    def nrm(shape, scale):
        return jax.random.normal(next(ks), shape, jnp.float32) * scale

    def gain(shape):
        return 1.0 + nrm(shape, 0.02)

    return {
        "x_prompt": nrm((BATCH, SEQ, D_MODEL), 1.0),
        "x_sample": nrm((DEC_BATCH, DEC_SEQ, D_MODEL), 1.0),
        "state_rwkv_S": nrm((L, DEC_BATCH, RW_HEADS, RW_HD, RW_HD), 1.0),
        "state_rwkv_shift": nrm((L, DEC_BATCH, RW_COLS), 1.0),
        "cache_mem_k": nrm((L, DEC_BATCH, N_MEM, XA_HEADS, XA_HD), 1.0),
        "cache_mem_v": nrm((L, DEC_BATCH, N_MEM, XA_HEADS, XA_HD), 1.0),
        "mem_prompt": nrm((BATCH, N_MEM, D_MODEL), 1.0),
        "norm1_g": gain((L, D_MODEL)),
        "w_in": nrm((L, D_MODEL, IN_COLS), D_MODEL ** -0.5),
        "gate_b": nrm((L, N_BRANCH * D_MODEL), 0.1),
        "gm_ln_g": gain((L, BRANCH_W)),
        "gm_ln_b": nrm((L, BRANCH_W), 0.02),
        "gm_ws": nrm((L, GM_GROUPS, CHUNK, CHUNK), CHUNK ** -0.5),
        "gm_bs": 1.0 + nrm((L, GM_GROUPS, CHUNK), 0.1),
        "rw_mu": jax.random.uniform(next(ks), (L, RW_COLS), jnp.float32, 0.0, 1.0),
        "rw_w0": jax.random.uniform(next(ks), (L, BRANCH_W), jnp.float32, -6.0, -1.0),
        "rw_w2": nrm((L, RW_W_LORA, BRANCH_W), 0.1),
        "rw_a0": nrm((L, BRANCH_W), 0.5),
        "rw_a2": nrm((L, RW_A_LORA, BRANCH_W), RW_A_LORA ** -0.5),
        "rw_g2": nrm((L, RW_G_LORA, BRANCH_W), RW_G_LORA ** -0.5),
        "rw_k_k": 0.85 + nrm((L, BRANCH_W), 0.1),
        "rw_k_a": 1.0 + nrm((L, BRANCH_W), 0.1),
        "rw_r_k": nrm((L, RW_HEADS, RW_HD), 0.1),
        "rw_lnx_g": gain((L, BRANCH_W)),
        "rw_lnx_b": nrm((L, BRANCH_W), 0.02),
        "xa_wk": nrm((L, D_MODEL, BRANCH_W), D_MODEL ** -0.5),
        "xa_wv": nrm((L, D_MODEL, BRANCH_W), D_MODEL ** -0.5),
        "w_branch": nrm((L, N_BRANCH, BRANCH_W, D_MODEL), BRANCH_W ** -0.5),
        "w_out": nrm((L, D_MODEL, D_MODEL), D_MODEL ** -0.5),
        "norm2_g": gain((L, D_MODEL)),
        "rg_w": nrm((L, D_MODEL, N_GROUPS), D_MODEL ** -0.5),
        "rg_b": nrm((L, N_GROUPS), 0.01),
        "re_w": nrm((L, N_GROUPS, D_MODEL, EXP_PER_GROUP), D_MODEL ** -0.5),
        "re_b": nrm((L, N_GROUPS, EXP_PER_GROUP), 0.01),
        "e_wg": nrm((L, N_GROUPS, EXP_PER_GROUP, D_MODEL, EXP_FF), D_MODEL ** -0.5),
        "e_wu": nrm((L, N_GROUPS, EXP_PER_GROUP, D_MODEL, EXP_FF), D_MODEL ** -0.5),
        "e_wd": nrm((L, N_GROUPS, EXP_PER_GROUP, EXP_FF, D_MODEL), EXP_FF ** -0.5),
        "final_g": gain((D_MODEL,)),
    }

def reference(x_prompt, x_sample, state_rwkv_S, state_rwkv_shift, cache_mem_k, cache_mem_v, mem_prompt,
              norm1_g, w_in, gate_b, gm_ln_g, gm_ln_b, gm_ws, gm_bs,
              rw_mu, rw_w0, rw_w2, rw_a0, rw_a2, rw_g2, rw_k_k, rw_k_a, rw_r_k, rw_lnx_g, rw_lnx_b,
              xa_wk, xa_wv, w_branch, w_out, norm2_g, rg_w, rg_b, re_w, re_b, e_wg, e_wu, e_wd, final_g):
    bp = x_prompt.shape[0]
    hp, hs = x_prompt, x_sample
    sp_list, shp_list, mkp_list, mvp_list = [], [], [], []
    ss_list, shs_list, vs_list = [], [], []
    for l in range(DEPTH):
        lw = (norm1_g[l], w_in[l], gate_b[l], gm_ln_g[l], gm_ln_b[l], gm_ws[l], gm_bs[l],
              rw_mu[l], rw_w0[l], rw_w2[l], rw_a0[l], rw_a2[l], rw_g2[l], rw_k_k[l], rw_k_a[l], rw_r_k[l],
              rw_lnx_g[l], rw_lnx_b[l], w_branch[l], w_out[l], norm2_g[l], rg_w[l], rg_b[l], re_w[l],
              re_b[l], e_wg[l], e_wu[l], e_wd[l])
        mk_p = (mem_prompt @ xa_wk[l]).reshape(bp, N_MEM, XA_HEADS, XA_HD)
        mv_p = (mem_prompt @ xa_wv[l]).reshape(bp, N_MEM, XA_HEADS, XA_HD)
        s0_p = jnp.zeros((bp, RW_HEADS, RW_HD, RW_HD), x_prompt.dtype)
        prev_p = jnp.zeros((bp, RW_COLS), x_prompt.dtype)
        hp, _, sp, shp = decoder_layer(hp, mk_p, mv_p, s0_p, prev_p, lw)
        hs, vs, ss, shs = decoder_layer(hs, cache_mem_k[l], cache_mem_v[l], state_rwkv_S[l],
                                        state_rwkv_shift[l], lw)
        sp_list.append(sp); shp_list.append(shp); mkp_list.append(mk_p); mvp_list.append(mv_p)
        ss_list.append(ss); shs_list.append(shs); vs_list.append(vs)
    y_prompt = rmsnorm(hp, final_g)
    y_sample = rmsnorm(hs, final_g)
    new_rwkv_S_prompt = jnp.stack(sp_list, axis=0)
    new_rwkv_shift_prompt = jnp.stack(shp_list, axis=0)
    new_mem_k_prompt = jnp.stack(mkp_list, axis=0)
    new_mem_v_prompt = jnp.stack(mvp_list, axis=0)
    new_rwkv_S_sample = jnp.stack(ss_list, axis=0)
    new_rwkv_shift_sample = jnp.stack(shs_list, axis=0)
    new_gmlp_v_sample = jnp.stack(vs_list, axis=0)
    return (y_prompt, y_sample, new_rwkv_S_prompt, new_rwkv_shift_prompt, new_mem_k_prompt, new_mem_v_prompt,
            new_rwkv_S_sample, new_rwkv_shift_sample, new_gmlp_v_sample)


_drawn_inputs = setup_inputs


def setup_inputs(seed=0):
    import zlib

    import numpy as np

    out = dict(_drawn_inputs(seed))
    spreads = {}
    factors = {'gm_ln_g': 7.383,
     'gm_ln_b': 7.485,
     'rw_lnx_g': 3.288,
     'rw_lnx_b': 3.275,
     'rg_b': 4.938,
     'final_g': 7.402,
     're_b': 4.22}
    for name, (base, spread) in spreads.items():
        noise = np.random.default_rng([zlib.crc32(name.encode()), seed]).standard_normal(out[name].shape)
        drawn = base * np.exp(spread * noise) if base else spread * noise
        out[name] = __import__('jax').numpy.asarray(drawn.astype(out[name].dtype))
    for name, factor in factors.items():
        out[name] = (out[name] * factor).astype(out[name].dtype)
    return out
```

```python
from contextlib import ExitStack

import concourse.bass as bass
import concourse.mybir as mybir
import numpy as np
from concourse.alu_op_type import AluOpType as ALU

ACT = mybir.ActivationFunctionType
AX = mybir.AxisListType
F32 = mybir.dt.float32
F32R = mybir.dt.float32r
I32 = mybir.dt.int32
U32 = mybir.dt.uint32

D = 1024
KD = D // 128
SEQ = 512
DB, DS = 8, 8
NS = DB * DS
NT = SEQ + NS
W = 512
NB = W // 128
TILES = [(128 * t, 128) for t in range(SEQ // 128)] + [(SEQ, NS)]
C = 64
NC = SEQ // C
RW = 3 * W + 256
RB = RW // 128
HD = 64
CH = 128
GG = 8
NM = 256
XH = 4
NG, NE = 4, 8
EX = NG * NE
FF = 512
CAP = 64
SPAN = 9
DECAY = float(np.exp(-0.5))
RMS_EPS, LN_EPS, GN_EPS = 1e-6, 1e-5, 64e-5
NOWHERE = 1 << 20
COL_U, COL_V, COL_R, COL_Q, COL_G = 0, W, 2 * W, 2 * W + RW, 3 * W + RW
P_MU, P_W0, P_A0, P_KK, P_KA, P_RK, P_GB, P_OK, P_END = 0, 14, 18, 22, 26, 30, 34, 58, 62


def await_round(engine, sem, value):
    value = engine.to_reg(value)
    engine.wait_ge(Steps.constant, 1)
    engine.wait_ge(sem, value)


class Steps:

    def __init__(self, sem, names, ahead=0):
        self.sem, self.names, self.at, self.ahead = sem, list(names), {}, ahead
        self.next = 0
        for n, name in enumerate(self.names):
            assert name not in self.at, name
            self.at[name] = n + 1

    def done(self, instruction, name):
        assert self.names[self.next % len(self.names)] == name, (self.names[self.next % len(self.names)], name)
        self.next += 1
        instruction.then_inc(self.sem, 1)

    def wait(self, engine, name, i=0):
        value = i * len(self.names) + (self.ahead * len(self.names) + self.at[name])
        if isinstance(i, int):
            engine.wait_ge(self.sem, value)
        else:
            await_round(engine, self.sem, value)

    def before(self, engine, name, i):
        await_round(engine, self.sem, i * len(self.names) + ((self.ahead - 1) * len(self.names) + self.at[name]))


class Sequence:

    def __init__(self, engine, sem):
        self.engine, self.sem, self.base, self.n = engine, sem, 0, 0
        self.per, self.rounds = 0, 0

    def __call__(self, instruction):
        self.n += 1
        instruction.then_inc(self.sem, 1)
        self.engine.wait_ge(self.sem, self.base + self.n)

    def enter(self, i, per):
        self.start, self.per = self.base + self.n, per
        self.base, self.n = i * per + self.start, 0

    def leave(self, rounds):
        assert self.n == self.per, f"{self.n} instructions in the body"
        self.base, self.n = self.start + rounds * self.per, 0


def unit_plan():
    chunks, units = [], []

    def add(kind, src, width, parts, tiles=KD):
        chunks.append((kind, src, width, tiles))
        step = width // parts
        for p in range(parts):
            n = sum(u[0] == kind for u in units)
            units.append((kind, n, len(chunks) - 1, p * step, (p + 1) * step, tiles))

    for c in range(3):
        add("rwkv", ("in", COL_R + c * W), W, 2)
    add("rwkv", ("in", COL_R + 3 * W), 256, 1)
    add("u", ("in", COL_U), W, 2)
    add("v", ("in", COL_V), W, 2)
    add("q", ("in", COL_Q), W, 2)
    add("wk", ("wk", 0), W, 2)
    add("wv", ("wv", 0), W, 2)
    for dp in range(D // 256):
        for b in range(3):
            add("merge", ("merge", (b, dp)), 256, 2, KD + NB)
    for c in range(D // W):
        add("out", ("out", c * W), W, 2)
    return chunks, units


def build(nc, x_prompt, x_sample, state_rwkv_S, state_rwkv_shift, cache_mem_k, cache_mem_v, mem_prompt,
          norm1_g, w_in, gate_b, gm_ln_g, gm_ln_b, gm_ws, gm_bs,
          rw_mu, rw_w0, rw_w2, rw_a0, rw_a2, rw_g2, rw_k_k, rw_k_a, rw_r_k, rw_lnx_g, rw_lnx_b,
          xa_wk, xa_wv, w_branch, w_out, norm2_g, rg_w, rg_b, re_w, re_b, e_wg, e_wu, e_wd, final_g,
          y_prompt, y_sample, S_prompt_out, shift_prompt_out, mem_k_out, mem_v_out,
          S_sample_out, shift_sample_out, gmlp_v_out):
    ctx = ExitStack()
    with ctx:
        cursor = [16640]

        def place(nbytes):
            at = cursor[0]
            cursor[0] += (nbytes + 63) // 64 * 64
            assert cursor[0] <= 229368, cursor[0]
            return at

        def sb(name, shape, dtype=F32, at=None):
            n = 4
            for s in shape[1:]:
                n *= s
            return nc.alloc_sbuf_tensor_at(name, shape, dtype, offset=place(n) if at is None else at)

        def sem(name):
            return ctx.enter_context(nc.semaphore(name))

        psum = [ctx.enter_context(nc.psum_tensor(f"bank{b}", [128, 512], F32)) for b in range(8)]

        ident = sb("ident", [128, 128])
        i64 = sb("i64", [128, 64])
        ones = sb("ones", [128, 128])
        before = sb("before", [128, 128])
        same_head = sb("same_head", [128, 128])
        low_s = sb("low_s", [128, 2, 64])
        up_s = sb("up_s", [128, 2, 64])
        up_i = sb("up_i", [128, 2, 64])
        own = sb("own", [128, DB])
        restart = sb("restart", [128, NT])
        par = sb("par", [128, P_END])
        bs_t = sb("bs_t", [128, GG])
        bs_s = sb("bs_s", [NS, GG])
        ssq = sb("ssq", [128, 8])
        rstd = sb("rstd", [128, 8])

        xnh_at = place(4 * KD * NT)
        xnl_at = place(4 * KD * NT)
        xnh = sb("xnh", [128, KD, NT], F32R, xnh_at)
        xnl = sb("xnl", [128, KD, NT], F32R, xnl_at)
        wh = sb("wh", [128, 3, 2048], F32R)
        wl = sb("wl", [128, 3, 2048], F32R)
        ring_at = place(0)
        ring = sb("ring", [128, 2, 4096])
        z = place(0)
        o_rw = sb("at_orw", [128, NB, NT], F32, z)
        o_gm = sb("bt_ogm", [128, NB, NT], F32, z + 9216)
        o_xa = sb("o_xa", [128, NB, NT], F32, z + 18432)
        z3 = z + 27648

        x_sb = sb("x_sb", [128, 5, D], F32, z3)
        g1b = sb("g1b", [128, D], F32, z3 + 20480)
        xq = sb("xq", [128, D], F32, z3 + 24576)
        rows = sb("rows", [P_GB + 24, 128], F32, z3 + 28672)
        okr = sb("bsn", [GG, 128], F32, z3 + 29184)
        pt = sb("pt", [128, RB, 585], F32, z + 18432)
        zs = z + 18432 + 4 * RB * 585 + 8
        shn = sb("shn", [DB, RW], F32, zs)
        sho = sb("sho", [9, RW], F32, zs + 7168)
        mix = [sb(f"mix{n}", [128, NT], F32, zs + 14336 + 2304 * n) for n in range(2)]
        w2 = sb("w2a2", [128, W], F32, zs + 18944)
        sig = sb("sig", [128, NB, NT], F32, zs)
        aa = sb("aa", [128, NB, NT], F32, zs + 9216)
        wa = sb("wa", [128, NT], F32, zs + 20992)
        tmp1 = sb("tmp1", [128, NT], F32, zs + 23296)
        tmp2 = sb("tmp2", [128, NT], F32, zs + 25600)
        wcp = sb("wcp", [128, NB, NC], F32, zs + 27904)
        wcs = sb("wcs", [128, NB, DB], F32, zs + 28032)
        bon = sb("bon", [128, NC + 1, NB], F32, zs + 28160)
        e1 = sb("e1", [128, NT], F32, zs + 18944)
        g2 = sb("g2", [128, W], F32, zs + 28352)
        cu = zs

        def chunk_buffer(name, shape):
            nonlocal cu
            n = 4
            for s in shape[1:]:
                n *= s
            t = sb(name, shape, F32, cu)
            cu += n
            return t

        ar = chunk_buffer("ar", [128, NB, 2, C])
        bc = chunk_buffer("bc", [128, NB, C])
        kc = chunk_buffer("kc", [128, NB, C])
        vc = chunk_buffer("vc", [128, NB, C])
        pm = chunk_buffer("pm", [128, NB, C])
        ptt = chunk_buffer("ptt", [128, NB, 2, C])
        rbt = chunk_buffer("rbt", [128, NB, C])
        mkt = chunk_buffer("mkt", [128, NB, C])
        rkt = chunk_buffer("rkt", [128, NB, C])
        vt = chunk_buffer("vt", [128, NB, C])
        bt = chunk_buffer("bt", [128, NB, C])
        kt = chunk_buffer("kt", [128, NB, C])
        gt = chunk_buffer("gt", [128, NB, C])
        xt = chunk_buffer("xt", [128, NB, C])
        ut = chunk_buffer("ut", [128, NB, C])
        st = chunk_buffer("st", [128, NB, C])
        yt = chunk_buffer("yt", [128, NB, C])
        ysq = chunk_buffer("ysq", [128, NB, C])
        bv = chunk_buffer("bv", [128, NB, C])
        sgc = chunk_buffer("sgc", [128, C])
        assert cu <= zs + 27904 - 1280, cu - zs
        mom = sb("mom", [128, 4, NB], F32, zs + 27904 - 1280)
        lnx = sb("lnx", [128, 2, NB, HD], F32, zs + 30464)
        s0n = sb("s0n", [128, DB, NB, HD], F32, ring_at)
        s0t = sb("s0t", [128, NB, DB, HD], F32, ring_at + 8192)
        big = [sb(f"big{n}", [128, DB, HD], F32, z + 18432 + 2048 * n) for n in range(4)]
        sout = sb("sout", [128, DB, NB, HD], F32, z + 18432 + 8192)

        ug = sb("ug", [128, 5, W], F32, z3)
        vg = sb("vg", [128, 5, W], F32, z3 + 10240)
        wn = sb("wn", [128, GG, CH], F32, z3 + 20480)
        wt = sb("wt", [128, GG, CH], F32, z3 + 24576)
        wsn = sb("wsn", [NS, GG, NS], F32, z3 + 28672)
        wst = sb("wst", [NS, GG, NS], F32, z3 + 30720)
        lng = sb("lng", [128, 2, W], F32, z3 + 32768)
        bst = sb("bst", [128, 5, 6], F32, z3 + 36864)
        mv = sb("mv", [128, 5, 2], F32, z3 + 36992)
        gtmp = sb("gtmp", [128, W], F32, z3 + 37056)
        qt = sb("qt", [128, XH, NT], F32, z3)
        mn = sb("mn", [128, 2, D], F32, z3 + 9216)
        qm = sb("qm", [128, XH, NT], F32, z3 + 9216)
        mth = sb("mth", [128, KD, NM], F32R, z3 + 18432)
        mtl = sb("mtl", [128, KD, NM], F32R, z3 + 26624)
        kvs = sb("kvs", [128, 4, 2, W], F32, z3 + 18432)
        kn = sb("kn", [128, 2, W], F32, z3 + 34816)
        vn = sb("vn", [128, 2, W], F32, z3 + 38912)
        ktm = sb("ktm", [128, XH, NM], F32, z3 + 43008)
        prob = sb("prob", [128, XH, NM], F32, z3 + 47104)
        prt = sb("prt", [128, XH * 2, 128], F32, z3 + 51200)
        smx = sb("smx", [128, 4, XH], F32, z3 + 55296)
        assert z3 + 55360 <= 229368
        oh = sb("oh", [128, 3 * NB, NT], F32R, z3)
        ol = sb("ol", [128, 3 * NB, NT], F32R, z3 + 27648)
        mt = sb("mt", [128, KD, NT], F32, z)
        gate = [sb(f"gate{n}", [128, NT], F32, z + 18432 + 2304 * n) for n in range(2)]
        prod = sb("prod", [128, NT], F32, z + 18432 + 4608)
        assert z3 + 55296 <= 229368
        mh = sb("mh", [128, KD, NT], F32R, xnh_at)
        ml = sb("ml", [128, KD, NT], F32R, xnl_at)
        h_at = z3
        h = sb("h", [128, 5, D], F32, h_at)


        slot_at = [ring_at, ring_at + 16384, xnh_at, xnh_at + 16384, z, z3 + 20480]
        slots = [sb(f"slot{n}", [128, 4096], F32, at) for n, at in enumerate(slot_at)]
        x2 = sb("x2", [128, 5, D], F32, z3 + 20480)
        xt2 = sb("xt2", [128, KD, NT], F32, z)
        g2b = sb("g2b", [128, D], F32, z + 18432)
        wr = sb("wr", [128, KD, NG + EX], F32, z + 22528)
        rb = sb("rb", [128, NG + EX], F32, z + 23680)
        cu = z3 + 40960

        def route_tile(name, shape, dtype=F32):
            nonlocal cu
            n = 4
            for s in shape[1:]:
                n *= s
            t = sb(name, shape, dtype, cu)
            cu += (n + 31) // 32 * 32
            return t

        lg = route_tile("lg", [128, 5, NG + EX])
        lg8 = route_tile("lg8", [128, 5, 8])
        les = route_tile("les", [128, 5, 8])
        le2 = route_tile("le2", [128, 5, 8])
        ltmp = route_tile("ltmp", [128, 5, 8])
        mx = [route_tile(f"mx{n}", [128, 5, 8]) for n in range(3)]
        mi = [route_tile(f"mi{n}", [128, 5, 8], U32) for n in range(3)]
        ix = route_tile("ix", [128, 3, 5])
        ohg = route_tile("ohg", [128, 5, NG])
        pex = route_tile("pex", [128, 5, NG])
        pg = route_tile("pg", [128, 8, 5])
        eid = route_tile("eid", [128, 2, 5])
        oh12 = route_tile("oh12", [128, 2, 5, EX])
        sel = route_tile("sel", [128, 5, EX])
        post = route_tile("post", [128, 5, EX])
        slot12 = route_tile("slot12", [128, 2, 5])
        iota_f = route_tile("iota_f", [128, EX])
        iota_i = route_tile("iota_i", [128, EX], I32)
        addr = route_tile("addr", [128, 2, 5], U32)
        val = route_tile("val", [128, 2, 5], I32)
        far = route_tile("far", [128, SPAN * CAP * EX // 128], I32)
        assert cu <= z3 + 54272
        xg = [sb(f"xg{n}", [CAP, D], F32, z + 16384 + 4096 * n) for n in range(2)]
        ht = sb("ht", [128, 4, CAP], F32, z + 24576)
        hs = sb("hs", [128, 4, 2 * CAP], F32R, z + 25600)
        xs = [sb("xs0", [128, KD, 2 * CAP], F32R, xnh_at + 32768), sb("xs1", [128, KD, 2 * CAP], F32R, z3 + 36864)]
        gs = sb("gs", [128, FF], F32, z3 + 40960)
        us = sb("us", [128, FF], F32, z3 + 43008)
        sg = sb("sg", [128, 4, CAP], F32, z3 + 45056)
        ym = sb("ym", [CAP, D], F32, z3 + 46080)
        yo = sb("yo", [CAP, D], F32, z3 + 50176)
        cu = z3 + 54272
        tab = route_tile("tab", [CAP, SPAN, EX], I32)
        tabg = route_tile("tabg", [CAP, SPAN, EX], I32)
        c12 = route_tile("c12", [128, 2, 5])
        cnt = route_tile("cnt", [128, EX])
        most = route_tile("most", [1, 1])
        most_i = route_tile("most_i", [1, 1], I32)
        ig = route_tile("ig", [CAP, 2], U32)
        is_ = route_tile("is_", [CAP, 2], U32)
        half = route_tile("half", [128, 64])
        assert cu <= 229368, cu
        fgb = sb("fgb", [128, D], F32, xnh_at + 32768)
        yb = [slots[2][:, 0:2048], slots[2][:, 2048:4096], slots[3][:, 0:2048], slots[3][:, 2048:4096], slots[4][:, 0:2048]]
        sqx = sb("sqx", [128, D], F32, z3 + 40960)
        xs32 = sb("xs32", [128, KD, CAP], F32, z3 + 36864)
        sg2 = sb("sg2", [CAP, FF], F32, z3 + 40960)
        h2 = sb("h2", [CAP, FF], F32, z3 + 43008)
        ht2 = sb("ht2", [128, 4, CAP], F32, z3 + 45056)
        xn2_d = nc.dram_tensor("normed_tokens", (NT, D), F32, kind="Internal").ap()
        y_d = nc.dram_tensor("expert_outputs", (2 * NT, D), F32, kind="Internal").ap()
        tab_d = nc.dram_tensor("token_lists", (SPAN * CAP * EX, 1), I32, kind="Internal").ap()
        chunks, units = unit_plan()
        RWKV_UNITS = 7
        kinds = [u[0] for u in units]
        first_unit = {k: kinds.index(k) for k in kinds}
        x_loaded, g1_loaded, par_loaded = sem("x_loaded"), sem("g1_loaded"), sem("par_loaded")
        rw_loaded, gm_loaded, diag_loaded, mem_loaded = sem("rw_loaded"), sem("gm_loaded"), sem("diag_loaded"), sem("mem_loaded")
        s0_loaded, x2_loaded = sem("s0_loaded"), sem("x2_loaded")
        kv_loaded = [sem(f"kv_loaded{n}") for n in range(4)]
        slot_loaded = [sem("slot0_loaded"), sem("slot1_loaded")]
        stored = sem("stored")
        pool_seq, act_seq, dve_seq = sem("pool_seq"), sem("act_seq"), sem("dve_seq")
        consts_ready = sem("consts_ready")
        Steps.constant = consts_ready
        hi_ready, lo_ready, unit_used = sem("hi_ready"), sem("lo_ready"), sem("unit_used")
        blocks_done = sem("blocks_done")
        state_ready = sem("state_ready")

        act_evac = Steps(sem("act_evac"), [u for u, k in enumerate(kinds) if k != "wv" and k != "out"])
        dve_evac = Steps(sem("dve_evac"), [u for u, k in enumerate(kinds) if k not in ("u", "v", "wk")])

        TG = [(t, g) for t in range(5) for g in range(2)]
        pe_n1 = Steps(sem("pe_n1"), ["par"] + [("turned", *tg) for tg in TG])
        act_n1 = Steps(sem("act_n1"), ["par", "bs"] + [("sq", t) for t in range(5)] + ["root"] + [("hi", *tg) for tg in TG])
        dve_n1 = Steps(sem("dve_n1"), ["clear", "ms"] + [("xn", t) for t in range(5)] + ["ok"] + [("lo", *tg) for tg in TG])

        pe_r = Steps(sem("pe_r"), ["shift_in", "shift_out0", "shift_out1", "shift_out2", "shift_out3"]
                     + [(w, b) for b in range(NB) for w in ("z", "a")] + [("heads", b) for b in range(NB)]
                     + [("bonus", b) for b in range(NB)])
        act_r = Steps(sem("act_r"), [("row", n) for n in range(4)] + [("pt", b) for b in range(RB)] + ["tanh", "ad", "gd"]
                      + [(w, b) for b in range(NB) for w in ("z", "a")] + [("sq", b) for b in range(NB)] + ["root"]
                      + [(w, b) for b in range(NB) for w in ("e1", "e2", "e3")])
        dve_r = Steps(sem("dve_r"), ["prev"] + [("mixed", b) for b in range(RB)]
                      + [("kk", b) for b in range(NB)] + [("cut", b) for b in range(NB)] + ["unit"]
                      + [(w, b) for b in range(NB) for w in ("sum", "less", "rk", "done")] + ["bonus"])
        LEVELS = [0, 1, 2, 3, 4, 5]
        PE_B = ["mt", "mk", "m", "turn"] + [("level", n) for n in LEVELS] + ["x", "u", "y", "s", "out"]
        ACT_B = ["ar", "rest", "turned"] + [("p", n) for n in LEVELS[:-1]] + ["x", "u", "y", "sq", "root"]
        DVE_B = ["copied", "masked"] + [("level", n) for n in LEVELS] + ["centred", "var", "o"]
        pe_b, act_b, dve_b = (Steps(sem(n), s) for n, s in (("pe_b", PE_B), ("act_b", ACT_B), ("dve_b", DVE_B)))
        pool_b = Steps(sem("pool_b"), ["bonus"])
        LEVELS_S = [0, 1, 2]
        pe_s = Steps(sem("pe_s"), ["sfin"] + [("s0", b) for b in range(NB)] + ["mt", "mk", "m", "turn"]
                     + [("level", n) for n in LEVELS_S] + [("xs", b) for b in range(NB)] + ["x", "u"]
                     + [("ys", b) for b in range(NB)] + ["y"] + [("sn", b) for b in range(NB)] + [("sb", b) for b in range(NB)] + ["out"])
        act_s = Steps(sem("act_s"), ["sfin"] + [("s0", b) for b in range(NB)] + ["ar", "rest", "turned"] + [("p", n) for n in LEVELS_S[:-1]]
                      + ["u", "sq", "root"] + [("sb", b) for b in range(NB)] + ["out"])
        dve_s = Steps(sem("dve_s"), ["copied", "masked"] + [("level", n) for n in LEVELS_S] + [("xs", b) for b in range(NB)] + ["x"]
                      + [("ys", b) for b in range(NB)] + [("spread", b) for b in range(NB)]
                      + ["centred", "var"] + [("sn", b) for b in range(NB)] + ["o"])
        pool_s = Steps(sem("pool_s"), ["bonus"])
        pe_g = Steps(sem("pe_g"), ["w0", "w1", "ws"] + [("s", t) for t in range(5)] + [("turned", t) for t in range(5)])
        act_g = Steps(sem("act_g"), ["w0", "w1", "ws", "root"] + [("o", t) for t in range(5)])
        dve_g = Steps(sem("dve_g"), ["var"] + [("vn", t) for t in range(5)] + [("o", t) for t in range(5)])
        pool_g = Steps(sem("pool_g"), ["zero", "causal"])
        MG = [(m, g) for m in range(2) for g in range(2)]
        pe_x = Steps(sem("pe_x"), [("mem", *x) for x in MG] + ["kt0", "kt1"]
                     + [(w, t) for t in range(4) for w in ("score", "turned", "o")]
                     + [("skt", b) for b in range(DB)] + ["sscore"] + ["sturned"])
        act_x = Steps(sem("act_x"), [("hi", *x) for x in MG] + ["kt0", "kt1"] + [(w, t) for t in range(4) for w in ("p", "turned", "o")]
                      + [("skt", b) for b in range(DB)] + ["sp", "sturned", "so"])
        pe_v = Steps(sem("pe_v"), [("v", b) for b in range(DB)])
        dve_x = Steps(sem("dve_x"), [("lo", *x) for x in MG] + [(w, t) for t in range(4) for w in ("max", "p", "turned")]
                      + ["qm"] + [("skt", b) for b in range(DB)] + ["smax", "sp", "sturned"])
        act_m = Steps(sem("act_m"), [("oh", n) for n in range(3)] + ["mh0", "mh1"])
        dve_m = Steps(sem("dve_m"), [("ol", n) for n in range(3)] + ["ml0", "ml1"])

        w_in_v = w_in[0].rearrange("(k p) n -> p k n", p=128)


        g2_loaded, wr_loaded, x2_stored, far_stored, listed = (sem(n) for n in ("g2_loaded", "wr_loaded", "x2_stored", "far_stored", "listed"))
        tab_loaded, fg_loaded, scattered = sem("tab_loaded"), sem("fg_loaded"), sem("scattered")
        eslot_loaded = [sem(f"eslot{n}_loaded") for n in range(6)]
        gathered = [sem("gathered0"), sem("gathered1")]
        yb_loaded = [sem(f"yb{t}_loaded") for t in range(5)]
        pe_t = Steps(sem("pe_t"), [("turned", *tg) for tg in TG] + ["logits", "pos"])
        act_t = Steps(sem("act_t"), [("sq", t) for t in range(5)] + ["root"] + [("xt", t) for t in range(5)] + ["exp_g", "exp_e"])
        dve_t = Steps(sem("dve_t"), ["clear", "ms"] + [("x2", t) for t in range(5)] + [("xt", t) for t in range(5)]
                      + ["lg", "dg", "de", "sel", "addr", "tab"])
        pool_t = Steps(sem("pool_t"), ["far", "iota", "xg"])
        UQ = range(6)
        pe_m = Steps(sem("pe_m"), [x for s in range(2) for x in [("t", s)] + [("unit", s, q) for q in range(4)] + [("gt", s)]
                                   + [("unit", s, q) for q in (4, 5)]], 1)
        act_e = Steps(sem("act_e"), [x for s in range(2) for x in [("hi", s, 0), ("xs", s), ("hi", s, 1), ("hi", s, 2), ("hi", s, 3),
                                     ("gs", s), ("hi", s, 4), ("hi", s, 5), ("silu", s), ("hs", s), ("ym", s)]], 1)
        dve_e = Steps(sem("dve_e"), [x for s in range(2) for x in [("lo", s, 0), ("xs", s), ("lo", s, 1), ("lo", s, 2), ("lo", s, 3),
                                     ("us", s), ("lo", s, 4), ("lo", s, 5), ("ht", s), ("hs", s), ("y", s)]], 1)
        pool_e = Steps(sem("pool_e"), [x for s in range(2) for x in [("ig", s), ("is", s)]], 1)
        act_f = Steps(sem("act_f"), [("sq", t) for t in range(5)] + ["root"])
        dve_f = Steps(sem("dve_f"), ["clear"] + [("sum", t) for t in range(5)] + ["ms"] + [("y", t) for t in range(5)])
        ROUNDS = EX // 2
        wgu = [w[0].rearrange("g e (k p) f -> (g e) p k f", p=128) for w in (e_wg, e_wu)]
        wdn = e_wd[0].rearrange("g e (k p) d -> (g e) p k d", p=128)

        def moe_sp(sp):
            def load(e, n):
                src = (wgu[n] if n < 2 else wdn)[bass.ds(e, 1)].rearrange("a p k f -> (a p) k f")
                return sp.dma_start(slots[n][:, :].rearrange("p (k n) -> p k n", k=8 if n < 2 else 4), src)

            dve_m.wait(sp, "ml1")
            sp.dma_start(g2b[:, :], norm2_g.to_broadcast([128, D])).then_inc(g2_loaded, 16)
            sp.dma_start(wr[:, :, 0:NG], rg_w[0].rearrange("(k p) n -> p k n", p=128)).then_inc(wr_loaded, 16)
            for g in range(NG):
                sp.dma_start(wr[:, :, NG + NE * g:NG + NE * g + NE], re_w[0, g].rearrange("(k p) n -> p k n", p=128))\
                    .then_inc(wr_loaded, 16)
            sp.dma_start(rb[:, 0:NG], rg_b.to_broadcast([128, NG])).then_inc(wr_loaded, 16)
            sp.dma_start(rb[:, NG:NG + EX], re_b.rearrange("a g e -> a (g e)").to_broadcast([128, EX])).then_inc(wr_loaded, 16)

            def first(s, n, slot):
                src = (wgu[n] if n < 2 else wdn)[s]
                sp.dma_start(slots[slot][:, :].rearrange("p (k n) -> p k n", k=8 if n < 2 else 4), src)\
                    .then_inc(eslot_loaded[slot], 16)

            sp.wait_ge(hi_ready, len(units))
            sp.wait_ge(lo_ready, len(units))
            first(0, 0, 0)
            first(0, 1, 1)
            sp.wait_ge(unit_used, len(units))
            first(0, 2, 2)
            first(1, 0, 3)
            for t, (t0, tn) in enumerate(TILES):
                dve_t.wait(sp, ("x2", t))
                sp.dma_start(xn2_d[t0:t0 + tn, :], x2[0:tn, t, :]).then_inc(x2_stored, 16)
            pool_t.wait(sp, "far")
            sp.dma_start(tab_d.rearrange("(p n) a -> p (n a)", p=128), far[:, :]).then_inc(far_stored, 16)
            sp.wait_ge(listed, 160)
            sp.dma_start(tab[:, :, :], tab_d.rearrange("(j s e) a -> s j (e a)", j=SPAN, s=CAP)).then_inc(tab_loaded, 16)
            sp.wait_ge(x2_stored, 80)
            pe_t.wait(sp, "pos")
            first(1, 1, 4)
            dve_t.wait(sp, "addr")
            first(1, 2, 5)
            with sp.Fori(0, ROUNDS - 1) as i:
                for s in range(2):
                    for n in range(3):
                        act_e.wait(sp, ("hi", s, 2 * n + 1), i)
                        dve_e.wait(sp, ("lo", s, 2 * n + 1), i)
                        src = (wgu[n] if n < 2 else wdn)[bass.ds(2 * i + (2 + s), 1)].rearrange("a p k f -> (a p) k f")
                        sp.dma_start(slots[3 * s + n][:, :].rearrange("p (k n) -> p k n", k=8 if n < 2 else 4), src)\
                            .then_inc(eslot_loaded[3 * s + n], 16)
            general_sp(sp)
            sp.wait_ge(scattered_all, 1)
            sp.dma_start(fgb[:, :], final_g.rearrange("(a d) -> a d", a=1).to_broadcast([128, D])).then_inc(fg_loaded, 16)
            for t, (t0, tn) in enumerate(TILES):
                sp.dma_start(yb[t][0:tn, :], y_d.rearrange("(n k) d -> n (k d)", k=2)[t0:t0 + tn, :]).then_inc(yb_loaded[t], 16)
            for t in range(4):
                dve_f.wait(sp, ("y", t))
                sp.dma_start(y_prompt[0, 128 * t:128 * t + 128, :], h[:, t, :]).then_inc(stored, 16)
            dve_f.wait(sp, ("y", 4))
            sp.dma_start(y_sample.rearrange("b t d -> (b t) d"), h[0:NS, 4, :]).then_inc(stored, 16)
            sp.wait_ge(stored, 16 * (6 + NB + 5))

        def moe_pe(pe):
            dve_evac.wait(pe, len(units) - 1)
            for n, (t, g) in enumerate(TG):
                tn = TILES[t][1]
                dve_t.wait(pe, ("x2", t))
                if t >= 2:
                    (act_t if g == 0 else dve_t).wait(pe, ("xt", t - 2))
                for k in range(4):
                    mm = pe.transpose(psum[n % 4][:, 128 * k:128 * k + tn],
                                      x2[0:tn, t, 512 * g + 128 * k:512 * g + 128 * k + 128], ident[0:tn, 0:tn])
                pe_t.done(mm, ("turned", t, g))
            pe.wait_ge(wr_loaded, 16 * 7)
            act_t.wait(pe, ("xt", 4))
            dve_t.wait(pe, ("xt", 4))
            for t, (t0, tn) in enumerate(TILES):
                for k in range(KD):
                    mm = pe.matmul(psum[4][0:tn, 36 * t:36 * t + 36], xt2[:, k, t0:t0 + tn], wr[:, k, :],
                                   start=(k == 0), stop=(k == KD - 1))
            pe_t.done(mm, "logits")
            dve_t.wait(pe, "sel")
            for t in range(5):
                for o in range(t + 1):
                    pe.matmul(psum[5][:, EX * t:EX * t + EX], (before if o == t else ones)[:, :], sel[:, o, :],
                              start=(o == 0), stop=(o == t))
            for o in range(5):
                mm = pe.matmul(psum[5][:, EX * 5:EX * 6], ones[:, :], sel[:, o, :], start=(o == 0), stop=(o == 4))
            pe_t.done(mm, "pos")
            dve_t.wait(pe, "addr")
            pe.sem_inc(pe_m.sem, len(pe_m.names))

            with pe.Fori(0, ROUNDS) as i:
                for s in range(2):
                    await_round(pe, gathered[s], 16 * i + 16)
                    for k in range(KD):
                        mm = pe.transpose(psum[6][:, CAP * k:CAP * k + CAP], xg[s][:, 128 * k:128 * k + 128], ident[0:CAP, 0:CAP])
                    pe_m.done(mm, ("t", s))
                    act_e.wait(pe, ("xs", s), i)
                    dve_e.wait(pe, ("xs", s), i)
                    for q in range(4):
                        dve_e.wait(pe, ("lo", s, q), i)
                        for k in range(KD):
                            for part in (wh, wl):
                                mm = pe.matmul(psum[q // 2][:, 256 * (q % 2):256 * (q % 2) + 256], xs[s][:, k, :],
                                               part[:, q % 3, 256 * k:256 * k + 256],
                                               start=(k == 0 and part is wh), stop=(k == KD - 1 and part is wl))
                        pe_m.done(mm, ("unit", s, q))
                    act_e.wait(pe, ("gs", s), i)
                    dve_e.wait(pe, ("us", s), i)
                    for b, src in ((2, gs), (3, us)):
                        for f in range(4):
                            mm = pe.matmul(psum[b][:, CAP * f:CAP * f + CAP], src[:, 128 * f:128 * f + 128], half[:, :],
                                           start=True, stop=True)
                    pe_m.done(mm, ("gt", s))
                    act_e.wait(pe, ("hs", s), i)
                    dve_e.wait(pe, ("hs", s), i)
                    if s == 0:
                        dve_e.before(pe, ("y", 1), i)
                    else:
                        dve_e.wait(pe, ("y", 0), i)
                    for q in (4, 5):
                        dve_e.wait(pe, ("lo", s, q), i)
                        for c in range(2):
                            for k in range(2):
                                for part in (wh, wl):
                                    mm = pe.matmul(psum[4 + c][:, :], hs[:, 2 * (q - 4) + k, :],
                                                   part[:, q % 3, 1024 * k + 512 * c:1024 * k + 512 * c + 512],
                                                   start=(q == 4 and k == 0 and part is wh), stop=(q == 5 and k == 1 and part is wl))
                        pe_m.done(mm, ("unit", s, q))
            general_pe(pe)

        def moe_act(act, seq):
            dve_t.wait(act, "clear")
            for t, (_, tn) in enumerate(TILES):
                if t >= 1:
                    act_t.wait(act, ("sq", t - 1))
                act_t.done(act.activation(x2[0:tn, t, :], h[0:tn, t, :], ACT.Square, accum_out=ssq[0:tn, t:t + 1]), ("sq", t))
            dve_t.wait(act, "ms")
            act_t.done(act.activation(rstd[:, 0:5], ssq[:, 0:5], ACT.Sqrt), "root")
            for t, (t0, tn) in enumerate(TILES):
                pe_t.wait(act, ("turned", t, 0))
                act_t.done(act.activation(xt2[:, 0:4, t0:t0 + tn],
                                          psum[2 * (t % 2)][:, :].rearrange("p (k n) -> p k n", n=128)[:, :, 0:tn], ACT.Copy), ("xt", t))
            dve_t.wait(act, "dg")
            act_t.done(act.activation(pex[:, :, :], pex[:, :, :], ACT.Exp), "exp_g")
            dve_t.wait(act, "de")
            act_t.done(act.activation(pg[:, 3, :], pg[:, 3, :], ACT.Exp), "exp_e")
            dve_t.wait(act, "addr")
            act.sem_inc(act_e.sem, len(act_e.names))

            with act.Fori(0, ROUNDS) as i:
                def hi(s, q):
                    if q % 2 == 0:
                        await_round(act, eslot_loaded[3 * s + q // 2], 16 * i + 16)
                    if q >= 3:
                        pe_m.wait(act, ("unit", s, q - 3), i)
                    elif s == 1:
                        pe_m.wait(act, ("unit", 0, q + 3), i)
                    else:
                        pe_m.before(act, ("unit", 1, q + 3), i)
                    act_e.done(act.activation(e_part(wh, q), e_raw(s, q), ACT.Copy), ("hi", s, q))

                for s in range(2):
                    hi(s, 0)
                    pe_m.wait(act, ("t", s), i)
                    act_e.done(act.activation(xs[s][:, :, 0:CAP], psum[6][:, :].rearrange("p (k n) -> p k n", n=CAP), ACT.Copy), ("xs", s))
                    for q in (1, 2, 3):
                        hi(s, q)
                    pe_m.wait(act, ("unit", s, 1), i)
                    act_e.done(act.activation(gs[:, :], psum[0][:, :], ACT.Copy), ("gs", s))
                    hi(s, 4)
                    hi(s, 5)
                    pe_m.wait(act, ("gt", s), i)
                    act_e.done(act.activation(sg[:, :, :], psum[2][:, 0:4 * CAP].rearrange("p (f n) -> p f n", n=CAP), ACT.Silu), ("silu", s))
                    dve_e.wait(act, ("ht", s), i)
                    act_e.done(act.activation(hs[:, :, 0:CAP], ht[:, :, :], ACT.Copy), ("hs", s))
                    pe_m.wait(act, ("unit", s, 5), i)
                    if s == 0:
                        dve_e.before(act, ("y", 1), i)
                    else:
                        dve_e.wait(act, ("y", 0), i)
                    act.activation(ym[:, 0:512], psum[4][CAP:2 * CAP, :], ACT.Copy)
                    act_e.done(act.activation(ym[:, 512:1024], psum[5][CAP:2 * CAP, :], ACT.Copy), ("ym", s))
            general_act(act)
            dve_f.wait(act, "clear")
            for t, (_, tn) in enumerate(TILES):
                dve_f.wait(act, ("sum", t))
                if t >= 1:
                    act_f.wait(act, ("sq", t - 1))
                act_f.done(act.activation(sqx[0:tn, :], h[0:tn, t, :], ACT.Square, accum_out=ssq[0:tn, t:t + 1]), ("sq", t))
            dve_f.wait(act, "ms")
            act_f.done(act.activation(rstd[:, 0:5], ssq[:, 0:5], ACT.Sqrt), "root")

        def e_raw(s, q):
            slot = slots[3 * s + q // 2]
            if q < 4:
                return slot[:, :].rearrange("p (k n) -> p k n", n=FF)[:, :, 256 * (q % 2):256 * (q % 2) + 256]
            return slot[:, 2048 * (q - 4):2048 * (q - 4) + 2048].rearrange("p (k n) -> p k n", n=256)

        def e_part(part, q):
            return part[:, q % 3, :].rearrange("p (k n) -> p k n", n=256)

        def moe_dve(dve, seq):
            dve_evac.wait(dve, len(units) - 1)
            seq(dve.memset(ssq[:, :], float(D)))
            dve_t.done(dve.memset(sel[:, :, :], 0.0), "clear")
            act_t.wait(dve, ("sq", 4))
            dve_t.done(dve.tensor_scalar(ssq[:, 0:5], ssq[:, 0:5], 1.0 / D, RMS_EPS, ALU.mult, ALU.add), "ms")
            act_t.wait(dve, "root")
            dve.wait_ge(g2_loaded, 16)
            seq(dve.reciprocal(rstd[:, 0:5], rstd[:, 0:5]))
            for t, (_, tn) in enumerate(TILES):
                dve_t.done(dve.scalar_tensor_tensor(x2[0:tn, t, :], h[0:tn, t, :], rstd[0:tn, t:t + 1], g2b[0:tn, :],
                                                    ALU.mult, ALU.mult), ("x2", t))
            for t, (t0, tn) in enumerate(TILES):
                pe_t.wait(dve, ("turned", t, 1))
                dve_t.done(dve.tensor_copy(xt2[:, 4:8, t0:t0 + tn],
                                           psum[2 * (t % 2) + 1][:, :].rearrange("p (k n) -> p k n", n=128)[:, :, 0:tn]), ("xt", t))
            pool_t.wait(dve, "iota")
            dve.wait_ge(x2_stored, 80)
            pe_t.wait(dve, "logits")
            seq(dve.memset(lg[:, :, :], 0.0))
            seq(dve.memset(lg8[:, :, :], -1e30))
            seq(dve.tensor_copy(iota_f[:, :], iota_i[:, :]))
            n36 = NG + EX
            dve.tensor_tensor(lg[:, 0:4, :], psum[4][:, 0:4 * n36].rearrange("p (t n) -> p t n", n=n36),
                              rb[:, :].unsqueeze(1).to_broadcast([128, 4, n36]), ALU.add)
            seq(dve.tensor_tensor(lg[0:NS, 4, :], psum[4][0:NS, 4 * n36:5 * n36], rb[0:NS, :], ALU.add))
            dve_t.done(dve.tensor_copy(lg8[:, :, 0:NG], lg[:, :, 0:NG]), "lg")
            dve_t.wait(dve, "lg")

            def top(src, n):
                for t in range(5):
                    last = dve.max(mx[n][:, t, :], src[:, t, :])
                seq(last)
                for t in range(5):
                    last = dve.max_index(mi[n][:, t, :], mx[n][:, t, :], src[:, t, :])
                seq(last)
                seq(dve.tensor_copy(ix[:, n, :], mi[n][:, :, 0]))

            def wide(ap, n):
                return ap.unsqueeze(2).to_broadcast([128, 5, n])

            def iota5(n):
                return iota_f[:, 0:n].unsqueeze(1).to_broadcast([128, 5, n])

            top(lg8, 0)
            seq(dve.tensor_tensor(ohg[:, :, :], iota5(NG), wide(ix[:, 0, :], NG), ALU.is_equal))
            dve_t.done(dve.tensor_tensor(pex[:, :, :], lg[:, :, 0:NG], wide(mx[0][:, :, 0], NG), ALU.subtract), "dg")
            seq(dve.tensor_tensor(les[:, :, :], lg[:, :, NG:NG + NE], wide(ohg[:, :, 0], NE), ALU.mult))
            for g in range(1, NG):
                seq(dve.tensor_tensor(ltmp[:, :, :], lg[:, :, NG + NE * g:NG + NE * g + NE], wide(ohg[:, :, g], NE), ALU.mult))
                seq(dve.tensor_tensor(les[:, :, :], les[:, :, :], ltmp[:, :, :], ALU.add))
            top(les, 1)
            seq(dve.tensor_tensor(ltmp[:, :, :], iota5(NE), wide(ix[:, 1, :], NE), ALU.is_equal))
            seq(dve.scalar_tensor_tensor(le2[:, :, :], ltmp[:, :, :], -1e30, les[:, :, :], ALU.mult, ALU.add))
            top(le2, 2)
            dve_t.done(dve.tensor_tensor(pg[:, 3, :], mx[2][:, :, 0], mx[1][:, :, 0], ALU.subtract), "de")
            act_t.wait(dve, "exp_g")
            seq(dve.tensor_reduce(pg[:, 0, :], pex[:, :, :], AX.X, ALU.add))
            seq(dve.reciprocal(pg[:, 1, :], pg[:, 0, :]))
            act_t.wait(dve, "exp_e")
            seq(dve.tensor_scalar(pg[:, 4, :], pg[:, 3, :], 1.0, None, ALU.add))
            seq(dve.reciprocal(pg[:, 5, :], pg[:, 4, :]))
            seq(dve.tensor_tensor(c12[:, 0, :], pg[:, 1, :], pg[:, 5, :], ALU.mult))
            dve.tensor_tensor(c12[:, 1, :], c12[:, 0, :], pg[:, 3, :], ALU.mult)
            for k in range(2):
                seq(dve.scalar_tensor_tensor(eid[:, k, :], ix[:, 0, :], float(NE), ix[:, 1 + k, :], ALU.mult, ALU.add))
                seq(dve.tensor_tensor(oh12[:, k, :, :], iota5(EX), wide(eid[:, k, :], EX), ALU.is_equal))
            dve.tensor_tensor(sel[:, 0:4, :], oh12[:, 0, 0:4, :], oh12[:, 1, 0:4, :], ALU.add)
            dve_t.done(dve.tensor_tensor(sel[0:NS, 4, :], oh12[0:NS, 0, 4, :], oh12[0:NS, 1, 4, :], ALU.add), "sel")
            pe_t.wait(dve, "pos")
            for k in range(2):
                seq(dve.tensor_tensor(post[:, :, :], oh12[:, k, :, :],
                                      psum[5][:, 0:5 * EX].rearrange("p (t e) -> p t e", e=EX), ALU.mult))
                seq(dve.tensor_reduce(slot12[:, k, :], post[:, :, :], AX.X, ALU.add))
            seq(dve.scalar_tensor_tensor(eid[:, :, :], slot12[:, :, :], float(EX), eid[:, :, :], ALU.mult, ALU.add))
            seq(dve.tensor_copy(cnt[:, :], psum[5][:, 5 * EX:6 * EX]))
            seq(dve.tensor_reduce(most[:, :], cnt[0:1, :], AX.X, ALU.max))
            seq(dve.tensor_copy(most_i[:, :], most[:, :]))
            dve_t.done(dve.tensor_copy(addr[:, :, :], eid[:, :, :]), "addr")
            dve.wait_ge(tab_loaded, 16)
            dve_t.done(dve.tensor_scalar(tabg[:, :, :], tab[:, :, :], 1, None, ALU.logical_shift_right), "tab")
            dve.sem_inc(dve_e.sem, len(dve_e.names))

            with dve.Fori(0, ROUNDS) as i:
                def lo(s, q):
                    act_e.wait(dve, ("hi", s, q), i)
                    dve_e.done(dve.tensor_tensor(e_part(wl, q), e_raw(s, q), e_part(wh, q).bitcast(F32), ALU.subtract), ("lo", s, q))

                for s in range(2):
                    lo(s, 0)
                    act_e.wait(dve, ("xs", s), i)
                    dve_e.done(dve.tensor_tensor(xs[s][:, :, CAP:2 * CAP], psum[6][:, :].rearrange("p (k n) -> p k n", n=CAP),
                                                 xs[s][:, :, 0:CAP].bitcast(F32), ALU.subtract), ("xs", s))
                    for q in (1, 2, 3):
                        lo(s, q)
                    pe_m.wait(dve, ("unit", s, 3), i)
                    dve_e.done(dve.tensor_copy(us[:, :], psum[1][:, :]), ("us", s))
                    lo(s, 4)
                    lo(s, 5)
                    act_e.wait(dve, ("silu", s), i)
                    dve_e.done(dve.tensor_tensor(ht[:, :, :], sg[:, :, :], psum[3][:, 0:4 * CAP].rearrange("p (f n) -> p f n", n=CAP),
                                                 ALU.mult), ("ht", s))
                    act_e.wait(dve, ("hs", s), i)
                    dve_e.wait(dve, ("ht", s), i)
                    dve_e.done(dve.tensor_tensor(hs[:, :, CAP:2 * CAP], ht[:, :, :], hs[:, :, 0:CAP].bitcast(F32), ALU.subtract), ("hs", s))
                    act_e.wait(dve, ("ym", s), i)
                    await_round(dve, scattered, 32 * i + 16 * (s + 1))
                    dve.tensor_tensor(yo[:, 0:512], ym[:, 0:512], psum[4][0:CAP, :], ALU.add)
                    dve_e.done(dve.tensor_tensor(yo[:, 512:1024], ym[:, 512:1024], psum[5][0:CAP, :], ALU.add), ("y", s))
            general_dve(dve)
            dve_f.done(dve.memset(ssq[:, :], float(D)), "clear")
            for t, (_, tn) in enumerate(TILES):
                dve.wait_ge(yb_loaded[t], 16)
                seq(dve.scalar_tensor_tensor(h[0:tn, t, :], yb[t][0:tn, 0:D], c12[0:tn, 0, t:t + 1], h[0:tn, t, :], ALU.mult, ALU.add))
                dve_f.done(dve.scalar_tensor_tensor(h[0:tn, t, :], yb[t][0:tn, D:2 * D], c12[0:tn, 1, t:t + 1], h[0:tn, t, :],
                                                    ALU.mult, ALU.add), ("sum", t))
            act_f.wait(dve, ("sq", 4))
            dve_f.done(dve.tensor_scalar(ssq[:, 0:5], ssq[:, 0:5], 1.0 / D, RMS_EPS, ALU.mult, ALU.add), "ms")
            act_f.wait(dve, "root")
            dve.wait_ge(fg_loaded, 16)
            seq(dve.reciprocal(rstd[:, 0:5], rstd[:, 0:5]))
            for t, (_, tn) in enumerate(TILES):
                dve_f.done(dve.scalar_tensor_tensor(h[0:tn, t, :], h[0:tn, t, :], rstd[0:tn, t:t + 1], fgb[0:tn, :],
                                                    ALU.mult, ALU.mult), ("y", t))

        def moe_pool(pool, seq):
            dve_t.wait(pool, ("x2", 4))
            for g in range(2):
                act_t.wait(pool, ("xt", 4))
            seq(pool.memset(half[:, :], 0.0))
            for p in (0, 64):
                seq(pool.affine_select(out=half[p:p + 64, :], in_=half[p:p + 64, :], compare_op=ALU.not_equal, fill=1.0, base=0,
                                       pattern=[[-1, 64]], channel_multiplier=1))
            pool.wait_ge(x2_stored, 80)
            pool_t.done(pool.memset(far[:, :], NOWHERE), "far")
            pool.iota(iota_i[:, :], [[1, EX]], base=0, channel_multiplier=0)
            pool_t.done(pool.iota(val[:, :, :], [[1, 2], [256, 5]], base=0, channel_multiplier=2), "iota")
            dve_t.wait(pool, "addr")
            pool_t.wait(pool, "iota")
            pool.wait_ge(far_stored, 16)
            for k in range(2):
                for t, (_, tn) in enumerate(TILES):
                    pool.indirect_dma_start(tab_d, bass.IndirectOffsetOnAxis(addr[0:tn, k, t:t + 1], 0), val[0:tn, k, t:t + 1], None)\
                        .then_inc(listed, 16)
            seq(pool.memset(xg[0][:, :], 0.0))
            pool_t.done(pool.memset(xg[1][:, :], 0.0), "xg")
            pool_t.wait(pool, "xg")
            dve_t.wait(pool, "tab")
            pool.sem_inc(pool_e.sem, len(pool_e.names))
            seq(pool.memset(yo[:, :], 0.0))
            seq(pool.memset(is_[:, :], NOWHERE))
            pool.indirect_dma_start(y_d, bass.IndirectOffsetOnAxis(is_[:, 0:1], 0), yo[:, :], None,
                                    bounds_check=2 * NT - 1, oob_is_err=False).then_inc(scattered, 16)

            def gather(s):
                pool.indirect_dma_start(xg[s][:, :], None, xn2_d, bass.IndirectOffsetOnAxis(ig[:, s:s + 1], 0),
                                        bounds_check=NT - 1, oob_is_err=False).then_inc(gathered[s], 16)

            seq(pool.tensor_copy(ig[:, 0:1], tabg[:, 0, 0:1]))
            gather(0)
            with pool.Fori(0, ROUNDS) as i:
                for s in range(2):
                    if s == 0:
                        pe_m.before(pool, ("t", 1), i)
                    else:
                        pe_m.wait(pool, ("t", 0), i)
                    pool_e.done(pool.tensor_copy(ig[:, 1 - s:2 - s], tabg[:, :, :].rearrange("p j e -> p (j e)")[:, bass.ds(2 * i + (s + 1), 1)]), ("ig", s))
                    pool_e.wait(pool, ("ig", s), i)
                    gather(1 - s)
                    await_round(pool, scattered, 32 * i + 16 * (s + 1))
                    pool_e.done(pool.tensor_copy(is_[:, s:s + 1], tab[:, :, :].rearrange("p j e -> p (j e)")[:, bass.ds(2 * i + s, 1)]), ("is", s))
                    pool_e.wait(pool, ("is", s), i)
                    dve_e.wait(pool, ("y", s), i)
                    pool.indirect_dma_start(y_d, bass.IndirectOffsetOnAxis(is_[:, s:s + 1], 0), yo[:, :], None,
                                            bounds_check=2 * NT - 1, oob_is_err=False).then_inc(scattered, 16)
            general_pool(pool)
            pool.memset(half[:, :], 0.0).then_inc(scattered_all, 1)

        scattered_all = sem("scattered_all")
        more_loaded, more_gathered, more_scattered = sem("more_loaded"), sem("more_gathered"), sem("more_scattered")
        pe_n = Steps(sem("pe_n"), ["t", "gu", "ht", "y"])
        act_n = Steps(sem("act_n"), ["xs", "silu", "ht"])
        dve_n = Steps(sem("dve_n"), ["h", "y"])
        pool_n = Steps(sem("pool_n"), ["index"])
        MORE = SPAN - 1

        def some_overflow(engine):
            return engine.value_load(most_i[0:1, 0:1], min_val=0, max_val=NT) > CAP

        def general_sp(sp):
            dve_e.wait(sp, ("y", 1), ROUNDS - 1)
            with sp.If(some_overflow(sp)):
                with sp.Fori(0, EX) as e:
                    for n in range(3):
                        src = (wgu[n] if n < 2 else wdn)[bass.ds(e, 1)].rearrange("a p k f -> (a p) k f")
                        sp.dma_start(slots[n][:, :].rearrange("p (k n) -> p k n", k=8 if n < 2 else 4), src).then_inc(more_loaded, 16)
                    pe_n.wait(sp, "y", MORE * e + (MORE - 1))

        def general_pe(pe):
            with pe.If(some_overflow(pe)):
                with pe.Fori(0, EX) as e:
                    with pe.Fori(0, MORE) as j:
                        r = MORE * e + j
                        await_round(pe, more_gathered, 16 * r + 16)
                        for k in range(KD):
                            mm = pe.transpose(psum[6][:, CAP * k:CAP * k + CAP], xg[0][:, 128 * k:128 * k + 128], ident[0:CAP, 0:CAP])
                        pe_n.done(mm, "t")
                        await_round(pe, more_loaded, 48 * e + 48)
                        act_n.wait(pe, "xs", r)
                        for n in range(2):
                            for k in range(KD):
                                mm = pe.matmul(psum[n][0:CAP, :], xs32[:, k, :], slots[n][:, FF * k:FF * k + FF],
                                               start=(k == 0), stop=(k == KD - 1))
                        pe_n.done(mm, "gu")
                        dve_n.wait(pe, "h", r)
                        for f in range(4):
                            mm = pe.transpose(psum[2][:, CAP * f:CAP * f + CAP], h2[:, 128 * f:128 * f + 128], ident[0:CAP, 0:CAP])
                        pe_n.done(mm, "ht")
                        act_n.wait(pe, "ht", r)
                        for c in range(2):
                            for f in range(4):
                                mm = pe.matmul(psum[4 + c][0:CAP, :], ht2[:, f, :], slots[2][:, D * f + 512 * c:D * f + 512 * c + 512],
                                               start=(f == 0), stop=(f == 3))
                        pe_n.done(mm, "y")

        def general_act(act):
            with act.If(some_overflow(act)):
                with act.Fori(0, EX) as e:
                    with act.Fori(0, MORE) as j:
                        r = MORE * e + j
                        pe_n.wait(act, "t", r)
                        act_n.done(act.activation(xs32[:, :, :], psum[6][:, :].rearrange("p (k n) -> p k n", n=CAP), ACT.Copy), "xs")
                        pe_n.wait(act, "gu", r)
                        act_n.done(act.activation(sg2[:, :], psum[0][0:CAP, :], ACT.Silu), "silu")
                        pe_n.wait(act, "ht", r)
                        act_n.done(act.activation(ht2[:, :, :], psum[2][:, 0:4 * CAP].rearrange("p (f n) -> p f n", n=CAP), ACT.Copy), "ht")

        def general_dve(dve):
            with dve.If(some_overflow(dve)):
                with dve.Fori(0, EX) as e:
                    with dve.Fori(0, MORE) as j:
                        r = MORE * e + j
                        act_n.wait(dve, "silu", r)
                        dve_n.done(dve.tensor_tensor(h2[:, :], sg2[:, :], psum[1][0:CAP, :], ALU.mult), "h")
                        pe_n.wait(dve, "y", r)
                        dve.tensor_copy(yo[:, 0:512], psum[4][0:CAP, :])
                        dve_n.done(dve.tensor_copy(yo[:, 512:1024], psum[5][0:CAP, :]), "y")

        def general_pool(pool):
            pool.wait_ge(scattered, 16 * (EX + 1))
            pool.wait_ge(gathered[0], 16 * (ROUNDS + 1))
            with pool.If(some_overflow(pool)):
                with pool.Fori(0, EX) as e:
                    with pool.Fori(0, MORE) as j:
                        r = MORE * e + j
                        at = bass.ds(EX * j + e + EX, 1)
                        pool.tensor_copy(ig[:, 0:1], tabg[:, :, :].rearrange("p j e -> p (j e)")[:, at])
                        pool_n.done(pool.tensor_copy(is_[:, 0:1], tab[:, :, :].rearrange("p j e -> p (j e)")[:, at]), "index")
                        pool_n.wait(pool, "index", r)
                        pool.indirect_dma_start(xg[0][:, :], None, xn2_d, bass.IndirectOffsetOnAxis(ig[:, 0:1], 0),
                                                bounds_check=NT - 1, oob_is_err=False).then_inc(more_gathered, 16)
                        dve_n.wait(pool, "y", r)
                        pool.indirect_dma_start(y_d, bass.IndirectOffsetOnAxis(is_[:, 0:1], 0), yo[:, :], None,
                                                bounds_check=2 * NT - 1, oob_is_err=False).then_inc(more_scattered, 16)
                        await_round(pool, more_scattered, 16 * r + 16)
        block = ctx.enter_context(nc.Block())

        @block.sync
        def _(sp):
            def chunk(j):
                kind, (what, where), width, _ = chunks[j]
                if j >= 2:
                    last = max(n for n, u in enumerate(units) if u[2] == j - 2)
                    sp.wait_ge(hi_ready, last + 1)
                    sp.wait_ge(lo_ready, last + 1)
                slot = ring[:, j % 2, :]
                if what == "merge":
                    b, dp = where
                    c = COL_G + b * D + dp * 256
                    sp.dma_start(slot[:, 0:KD * 256].rearrange("p (k n) -> p k n", n=256),
                                 w_in_v[:, :, c:c + 256]).then_inc(slot_loaded[j % 2], 16)
                    sp.dma_start(slot[:, KD * 256:(KD + NB) * 256].rearrange("p (k n) -> p k n", n=256),
                                 w_branch[0, b].rearrange("(k p) n -> p k n", p=128)[:, :, dp * 256:dp * 256 + 256])\
                        .then_inc(slot_loaded[j % 2], 16)
                    return
                src = {"in": w_in[0], "wk": xa_wk[0], "wv": xa_wv[0], "out": w_out[0]}[what]
                sp.dma_start(slot[:, 0:KD * width].rearrange("p (k n) -> p k n", n=width),
                             src.rearrange("(k p) n -> p k n", p=128)[:, :, where:where + width])\
                    .then_inc(slot_loaded[j % 2], 16)

            def store(out, in_):
                sp.dma_start(out, in_).then_inc(stored, 16)

            for t in range(4):
                sp.dma_start(x_sb[:, t, :], x_prompt[0, 128 * t:128 * t + 128, :]).then_inc(x_loaded, 16)
            sp.dma_start(x_sb[0:NS, 4, :], x_sample.rearrange("b t d -> (b t) d")).then_inc(x_loaded, 16)
            sp.dma_start(g1b[:, :], norm1_g.to_broadcast([128, D])).then_inc(g1_loaded, 16)
            for at, src in ((P_MU, rw_mu), (P_W0, rw_w0), (P_A0, rw_a0), (P_KK, rw_k_k), (P_KA, rw_k_a),
                            (P_RK, rw_r_k.rearrange("a h n -> a (h n)")), (P_GB, gate_b)):
                v = src.rearrange("a (c p) -> (a c) p", p=128)
                sp.dma_start(rows[at:at + v.shape[0], :], v).then_inc(par_loaded, 16)
            sp.dma_start(okr[:, :], gm_bs[0]).then_inc(par_loaded, 16)
            chunk(0)
            chunk(1)
            for b in range(DB):
                sp.dma_start(bs_s[DS * b:DS * b + DS, :], gm_bs[0, :, 0:DS].rearrange("g t -> t g"),
                             allow_slow_non_contiguous=True).then_inc(gm_loaded, 16)
            dve_n1.wait(sp, ("lo", 4, 1))
            sp.dma_start(shn[:, :], state_rwkv_shift[0]).then_inc(rw_loaded, 16)
            sp.dma_start(w2[0:64, :], rw_w2[0]).then_inc(rw_loaded, 16)
            sp.dma_start(w2[64:128, :], rw_a2[0]).then_inc(rw_loaded, 16)
            sp.dma_start(g2[:, :], rw_g2[0]).then_inc(rw_loaded, 16)
            for n, src in enumerate((rw_lnx_g, rw_lnx_b)):
                v = src.rearrange("a (k h i) -> a h k i", h=2, i=HD)
                for p in range(2):
                    sp.dma_start(lnx[64 * p:64 * p + 64, n, :, :], v[:, p].to_broadcast([64, NB, HD])).then_inc(rw_loaded, 16)
            chunk(2)
            chunk(3)
            act_r.wait(sp, ("row", 3))
            store(shift_prompt_out[0], sho[0:1, :])
            store(shift_sample_out[0], sho[1:9, :])
            sp.wait_ge(hi_ready, RWKV_UNITS)
            sp.wait_ge(lo_ready, RWKV_UNITS)
            for k in range(NB):
                sp.dma_start(s0n[:, :, k, :],
                             state_rwkv_S[0, :, 2 * k:2 * k + 2].rearrange("b p i j -> (p i) b j")).then_inc(s0_loaded, 16)
            act_s.wait(sp, "sfin")
            store(S_prompt_out[0, 0].rearrange("(k p) i j -> (p i) k j", p=2), st[:, :, :])
            for k in range(NB):
                act_s.wait(sp, ("sb", k))
                store(S_sample_out[0, :, 2 * k:2 * k + 2].rearrange("b p i j -> (p i) b j"), sout[:, :, k, :])
            dve_s.wait(sp, ("sn", NB - 1))
            chunk(4)
            chunk(5)
            act_s.wait(sp, "out")
            sp.wait_ge(stored, 16 * (3 + NB))
            sp.dma_start(wn[:, :, :], gm_ws[0].rearrange("g t s -> t g s")).then_inc(gm_loaded, 16)
            sp.dma_start(lng[:, 0, :], gm_ln_g.to_broadcast([128, W])).then_inc(gm_loaded, 16)
            sp.dma_start(lng[:, 1, :], gm_ln_b.to_broadcast([128, W])).then_inc(gm_loaded, 16)
            pool_g.wait(sp, "zero")
            for b in range(DB):
                sp.dma_start(wsn[DS * b:DS * b + DS, :, DS * b:DS * b + DS],
                             gm_ws[0, :, 0:DS, 0:DS].rearrange("g t s -> t g s")).then_inc(diag_loaded, 16)
            chunk(6)
            chunk(7)
            dve_g.wait(sp, ("vn", 4))
            store(gmlp_v_out[0].rearrange("b t w -> (b t) w"), vg[0:NS, 4, :])
            act_g.wait(sp, ("o", 4))
            sp.wait_ge(stored, 16 * (4 + NB))
            for m in range(2):
                sp.dma_start(mn[:, m, :], mem_prompt[0, 128 * m:128 * m + 128, :]).then_inc(mem_loaded, 16)
            chunk(8)
            act_evac.wait(sp, first_unit["wk"] + 1)
            store(mem_k_out[0, 0].rearrange("(m p) h d -> p m (h d)", p=128), kn[:, :, :])
            chunk(9)
            dve_evac.wait(sp, first_unit["wv"] + 1)
            store(mem_v_out[0, 0].rearrange("(m p) h d -> p m (h d)", p=128), vn[:, :, :])
            for n in range(2 * DB):
                src = (cache_mem_k if n < DB else cache_mem_v)[0, n % DB].rearrange("(m p) h d -> p m (h d)", p=128)
                if n == 0:
                    sp.wait_ge(unit_used, first_unit["wv"] + 2)
                if n >= 4:
                    if n - 4 < DB:
                        pe_x.wait(sp, ("skt", n - 4))
                    else:
                        pe_v.wait(sp, ("v", n - 4 - DB))
                sp.dma_start(kvs[:, n % 4, :, :], src).then_inc(kv_loaded[n % 4], 16)
            for j in range(10, len(chunks)):
                chunk(j)
            sp.wait_ge(unit_used, first_unit["out"])
            for t in range(4):
                sp.dma_start(h[:, t, :], x_prompt[0, 128 * t:128 * t + 128, :]).then_inc(x2_loaded, 16)
            sp.dma_start(h[0:NS, 4, :], x_sample.rearrange("b t d -> (b t) d")).then_inc(x2_loaded, 16)
            moe_sp(sp)

        @block.tensor
        def _(pe):
            def unit(u):
                kind, n, _, c0, c1, tiles = units[u]
                banks = psum[3 * (u % 2):3 * (u % 2) + 3]
                whi, wlo = (t[:, u % 3, :] for t in (wh, wl))
                pe.wait_ge(lo_ready, u + 1)
                for e in (act_evac, dve_evac):
                    if u >= 2 and u - 2 in e.at:
                        e.wait(pe, u - 2)
                if kind in ("rwkv", "q", "merge"):
                    def rows(tile0, wcols, nk, xh_, xl_, out512, out64):
                        for part, cols in ((out512, slice(0, SEQ)), (out64, slice(SEQ, NT))):
                            for k in range(nk):
                                w_h = whi[:, (tile0 + k) * (c1 - c0) + wcols:(tile0 + k) * (c1 - c0) + wcols + 128]
                                w_l = wlo[:, (tile0 + k) * (c1 - c0) + wcols:(tile0 + k) * (c1 - c0) + wcols + 128]
                                pe.matmul(part, w_h, xh_(k, cols), start=(k == 0), stop=False)
                                pe.matmul(part, w_h, xl_(k, cols), start=False, stop=False)
                                mm = pe.matmul(part, w_l, xh_(k, cols), start=False, stop=(k == nk - 1))
                        return mm

                    def xn_(t):
                        return lambda k, cols: t[:, k, cols]

                    if kind == "merge":
                        b = (n // 2) % 3
                        rows(0, 0, KD, xn_(xnh), xn_(xnl), banks[0][:, :], banks[2][:, 0:NS])
                        mm = rows(KD, 0, NB, lambda k, c: oh[:, NB * b + k, c], lambda k, c: ol[:, NB * b + k, c],
                                  banks[1][:, :], banks[2][:, NS:2 * NS])
                    else:
                        for m in range(2):
                            mm = rows(0, 128 * m, KD, xn_(xnh), xn_(xnl), banks[m][:, :],
                                      banks[2][:, NS * m:NS * m + NS])
                elif kind in ("u", "v", "out"):
                    hi_, lo_ = (mh, ml) if kind == "out" else (xnh, xnl)
                    for t, (t0, tn) in enumerate(TILES):
                        out = banks[t // 2][0:tn, 256 * (t % 2):256 * (t % 2) + 256]
                        for k in range(KD):
                            w_h, w_l = whi[:, 256 * k:256 * k + 256], wlo[:, 256 * k:256 * k + 256]
                            pe.matmul(out, hi_[:, k, t0:t0 + tn], w_h, start=(k == 0), stop=False)
                            pe.matmul(out, lo_[:, k, t0:t0 + tn], w_h, start=False, stop=False)
                            mm = pe.matmul(out, hi_[:, k, t0:t0 + tn], w_l, start=False, stop=(k == KD - 1))
                else:
                    for m in range(2):
                        out = banks[0][:, 256 * m:256 * m + 256]
                        for k in range(KD):
                            w_h, w_l = whi[:, 256 * k:256 * k + 256], wlo[:, 256 * k:256 * k + 256]
                            pe.matmul(out, mth[:, k, 128 * m:128 * m + 128], w_h, start=(k == 0), stop=False)
                            pe.matmul(out, mtl[:, k, 128 * m:128 * m + 128], w_h, start=False, stop=False)
                            mm = pe.matmul(out, mth[:, k, 128 * m:128 * m + 128], w_l, start=False, stop=(k == KD - 1))
                mm.then_inc(unit_used, 1)

            def units_of(*kinds_):
                for u, k in enumerate(kinds):
                    if k in kinds_:
                        unit(u)

            pe.wait_ge(consts_ready, 1)
            pe.wait_ge(par_loaded, 16 * 8)
            npar = P_GB + 24
            pe.transpose(psum[7][:, 0:npar], rows[0:npar, :], ident[0:npar, 0:npar])
            pe_n1.done(pe.transpose(psum[7][:, 64:64 + GG], okr[:, :], ident[0:GG, 0:GG]), "par")
            for n, (t, g) in enumerate(TG):
                dve_n1.wait(pe, ("xn", t))
                if n >= 7:
                    dve_n1.wait(pe, ("lo", *TG[n - 7]))
                tn = TILES[t][1]
                for k in range(4):
                    mm = pe.transpose(psum[n % 7][:, 128 * k:128 * k + tn],
                                      x_sb[0:tn, t, 512 * g + 128 * k:512 * g + 128 * k + 128], ident[0:tn, 0:tn])
                pe_n1.done(mm, ("turned", t, g))
            dve_n1.wait(pe, ("lo", 4, 1))
            act_n1.wait(pe, "bs")

            pe.wait_ge(rw_loaded, 16 * 8)
            for b in range(RB):
                mm = pe.transpose(psum[6][:, DB * b:DB * b + DB], shn[:, 128 * b:128 * b + 128], ident[0:DB, 0:DB])
            pe_r.done(mm, "shift_in")
            units_of("rwkv")
            act_evac.wait(pe, RWKV_UNITS - 1)
            dve_evac.wait(pe, RWKV_UNITS - 1)
            for n in range(4):
                for b in range(4 * n, min(4 * n + 4, RB)):
                    mm = pe.transpose(psum[n][0:9, 128 * (b % 4):128 * (b % 4) + 128], pt[:, b, 512:585:9], ident[:, :])
                pe_r.done(mm, f"shift_out{n}")
            act_r.wait(pe, "ad")
            act_r.wait(pe, ("row", 3))
            for b in range(NB):
                if b >= 2:
                    act_r.wait(pe, ("a", b - 2))
                for w, p in (("z", 0), ("a", 64)):
                    n = 4 + 2 * (b % 2) + p // 64
                    pe.matmul(psum[n][:, :], w2[p:p + 64, 128 * b:128 * b + 128], wa[p:p + 64, 0:SEQ], start=True, stop=True)
                    mm = pe.matmul(psum[n - 4][:, 0:NS], w2[p:p + 64, 128 * b:128 * b + 128], wa[p:p + 64, SEQ:NT],
                                   start=True, stop=True)
                    pe_r.done(mm, (w, b))
            act_r.wait(pe, ("a", NB - 1))
            for b in range(NB):
                act_r.wait(pe, ("sq", b))
                if b >= 2:
                    dve_r.wait(pe, ("cut", b - 2))
                n = 4 + 2 * (b % 2)
                pe.matmul(psum[n][:, :], same_head[:, :], o_gm[:, b, 0:SEQ], start=True, stop=True)
                mm = pe.matmul(psum[n + 1][:, 0:NS], same_head[:, :], o_gm[:, b, SEQ:NT], start=True, stop=True)
                pe_r.done(mm, ("heads", b))
            for b in range(NB):
                dve_r.wait(pe, ("rk", b))
                for c in range(NC + 1):
                    for p in (0, 64):
                        mm = pe.matmul(psum[0][p:p + 64, NB * c + b:NB * c + b + 1],
                                       sig[p:p + 64, b, C * c:C * c + C], ones[p:p + 64, 0:1], start=True, stop=True)
                pe_r.done(mm, ("bonus", b))
            dve_r.wait(pe, "bonus")

            def each_head():
                for b in range(NB):
                    for p in (0, 64):
                        yield b, slice(p, p + 64)

            def scores(pe_t, act_t, i, sample):
                act_t.wait(pe, "ar", i)
                act_t.wait(pe, "rest", i)
                dve_c = dve_s if sample else dve_b
                dve_c.wait(pe, "copied", i)
                for b, q in each_head():
                    mm = pe.matmul(psum[0][q, 128 * b:128 * b + 128], bc[q, b, :], ar[q, b, :, :], start=True, stop=True)
                pe_t.done(mm, "mt")
                for b, q in each_head():
                    mm = pe.matmul(psum[1][q, 128 * b:128 * b + 128], kc[q, b, :], ar[q, b, :, :], start=True, stop=True)
                pe_t.done(mm, "mk")
                for b, q in each_head():
                    mm = pe.matmul(psum[2][q, 64 * b:64 * b + 64], ar[q, b, 0, :], bc[q, b, :], start=True, stop=True)
                pe_t.done(mm, "m")
                for src, bank, col in ((vc, 3, 0), (bc, 3, 256), (kc, 4, 0)):
                    for b, q in each_head():
                        pe.matmul(psum[bank][q, col + 64 * b:col + 64 * b + 64], src[q, b, :], i64[q, :], start=True, stop=True)
                for p in (0, 64):
                    mm = pe.matmul(psum[4][p:p + 64, 256:512], sgc[:, :],
                                   g2[:, :].rearrange("k (b h i) -> k h b i", h=2, i=HD)[:, p // 64], start=True, stop=True)
                pe_t.done(mm, "turn")
                levels = LEVELS_S if sample else LEVELS
                for n in levels:
                    dve_c.wait(pe, "masked" if n == 0 else ("level", n - 1), i)
                    if n > 0:
                        act_t.wait(pe, ("p", n - 1), i)
                    last = n == levels[-1]
                    for b, q in each_head():
                        if not last:
                            pe.matmul(psum[5][q, 64 * b:64 * b + 64], ptt[q, b, 0, :], pm[q, b, :], start=True, stop=True)
                        if n == 0:
                            mm = pe.matmul(psum[0][q, 128 * b:128 * b + 64], pm[q, b, :], ptt[q, b, 0, :], start=True, stop=True)
                        elif last:
                            mm = pe.matmul(psum[0][q, 128 * b + 64:128 * b + 128], pm[q, b, :], ptt[q, b, 1, :], start=True, stop=True)
                        else:
                            mm = pe.matmul(psum[0][q, 128 * b:128 * b + 128], pm[q, b, :], ptt[q, b, :, :], start=True, stop=True)
                    pe_t.done(mm, ("level", n))

            with pe.Fori(0, NC) as i:
                scores(pe_b, act_b, i, False)
                dve_b.wait(pe, ("level", LEVELS[-1]), i)
                act_b.wait(pe, "turned", i)
                await_round(pe, state_ready, i + 1)
                for b, q in each_head():
                    pe.matmul(psum[5][q, 64 * b:64 * b + 64], ar[q, b, 0, :], st[q, b, :], start=True, stop=False)
                    mm = pe.matmul(psum[5][q, 64 * b:64 * b + 64], mkt[q, b, :], vt[q, b, :], start=False, stop=True)
                pe_b.done(mm, "x")
                act_b.wait(pe, "x", i)
                for b, q in each_head():
                    mm = pe.matmul(psum[6][q, 64 * b:64 * b + 64], ptt[q, b, 1, :], xt[q, b, :], start=True, stop=True)
                pe_b.done(mm, "u")
                act_b.wait(pe, "u", i)
                for b, q in each_head():
                    pe.matmul(psum[7][q, 64 * b:64 * b + 64], ar[q, b, 1, :], st[q, b, :], start=True, stop=False)
                    pe.matmul(psum[7][q, 64 * b:64 * b + 64], rbt[q, b, :], ut[q, b, :], start=False, stop=False)
                    mm = pe.matmul(psum[7][q, 64 * b:64 * b + 64], rkt[q, b, :], vt[q, b, :], start=False, stop=True)
                pe_b.done(mm, "y")
                for b, q in each_head():
                    pe.matmul(psum[6][q, 64 * b:64 * b + 64], bt[q, b, :], ut[q, b, :], start=True, stop=False)
                    mm = pe.matmul(psum[6][q, 64 * b:64 * b + 64], kt[q, b, :], vt[q, b, :], start=False, stop=True)
                pe_b.done(mm, "s")
                dve_b.wait(pe, "o", i)
                for b, q in each_head():
                    mm = pe.matmul(psum[7][q, 256 + 64 * b:320 + 64 * b], yt[q, b, :], i64[q, :], start=True, stop=True)
                pe_b.done(mm, "out")

            pe.wait_ge(state_ready, NC + 1)
            pe.wait_ge(blocks_done, NC + 1)
            for b, q in each_head():
                mm = pe.matmul(psum[7][q, 64 * b:64 * b + 64], st[q, b, :], i64[q, :], start=True, stop=True)
            pe_s.done(mm, "sfin")
            pe.wait_ge(s0_loaded, 16 * NB)
            for b in range(NB):
                for p in (0, 64):
                    for s in range(DB):
                        mm = pe.matmul(psum[1 + b][p:p + 64, 64 * s:64 * s + 64], s0n[p:p + 64, s, b, :],
                                       i64[p:p + 64, :], start=True, stop=True)
                pe_s.done(mm, ("s0", b))
            act_s.wait(pe, ("s0", NB - 1))
            scores(pe_s, act_s, 0, True)
            dve_s.wait(pe, ("level", LEVELS_S[-1]))
            act_s.wait(pe, "turned")
            for b in range(NB):
                for p in (0, 64):
                    mm = pe.matmul(psum[1 + b][p:p + 64, :], ar[p:p + 64, b, 0, :], s0t[p:p + 64, b, :, :], start=True, stop=True)
                pe_s.done(mm, ("xs", b))
            for b, q in each_head():
                mm = pe.matmul(psum[5][q, 64 * b:64 * b + 64], mkt[q, b, :], vt[q, b, :], start=True, stop=True)
            pe_s.done(mm, "x")
            dve_s.wait(pe, "x")
            for b, q in each_head():
                mm = pe.matmul(psum[6][q, 64 * b:64 * b + 64], ptt[q, b, 1, :], xt[q, b, :], start=True, stop=True)
            pe_s.done(mm, "u")
            for b in range(NB):
                for p in (0, 64):
                    mm = pe.matmul(psum[1 + b][p:p + 64, :], ar[p:p + 64, b, 1, :], s0t[p:p + 64, b, :, :], start=True, stop=True)
                pe_s.done(mm, ("ys", b))
            act_s.wait(pe, "u")
            for b, q in each_head():
                pe.matmul(psum[7][q, 64 * b:64 * b + 64], rbt[q, b, :], ut[q, b, :], start=True, stop=False)
                mm = pe.matmul(psum[7][q, 64 * b:64 * b + 64], rkt[q, b, :], vt[q, b, :], start=False, stop=True)
            pe_s.done(mm, "y")
            dve_s.wait(pe, ("ys", NB - 1))
            for b in range(NB):
                dve_s.wait(pe, ("spread", b))
                for p in (0, 64):
                    pe.matmul(psum[1 + b][p:p + 64, :], bt[p:p + 64, b, :], big[2 * (b % 2)][p:p + 64, :, :], start=True, stop=False)
                    mm = pe.matmul(psum[1 + b][p:p + 64, :], kt[p:p + 64, b, :], big[2 * (b % 2) + 1][p:p + 64, :, :],
                                   start=False, stop=True)
                pe_s.done(mm, ("sn", b))
            for b in range(NB):
                dve_s.wait(pe, ("sn", b))
                for p in (0, 64):
                    for s in range(DB):
                        mm = pe.matmul(psum[1 + b][p:p + 64, 64 * s:64 * s + 64], s0t[p:p + 64, b, s, :],
                                       i64[p:p + 64, :], start=True, stop=True)
                pe_s.done(mm, ("sb", b))
            dve_s.wait(pe, "o")
            for b, q in each_head():
                mm = pe.matmul(psum[7][q, 256 + 64 * b:320 + 64 * b], yt[q, b, :], i64[q, :], start=True, stop=True)
            pe_s.done(mm, "out")
            act_s.wait(pe, "out")

            units_of("u", "v")
            act_evac.wait(pe, first_unit["v"] + 1)
            pool_g.wait(pe, "causal")
            for n in range(2):
                for g in range(4):
                    mm = pe.transpose(psum[n][:, 128 * g:128 * g + 128], wn[:, 4 * n + g, :], ident[:, :])
                pe_g.done(mm, f"w{n}")
            for g in range(GG):
                mm = pe.transpose(psum[2][0:NS, NS * g:NS * g + NS], wsn[:, g, :], ident[0:NS, 0:NS])
            pe_g.done(mm, "ws")
            act_g.wait(pe, "ws")
            for t, (t0, tn) in enumerate(TILES):
                dve_g.wait(pe, ("vn", t))
                lhs = wst if t == 4 else wt
                for g in range(GG):
                    mm = pe.matmul(psum[3 + t][0:tn, HD * g:HD * g + HD], lhs[0:tn, g, 0:tn],
                                   vg[0:tn, t, HD * g:HD * g + HD], start=True, stop=True)
                pe_g.done(mm, ("s", t))
            for t, (t0, tn) in enumerate(TILES):
                dve_g.wait(pe, ("o", t))
                if t >= 3:
                    act_g.wait(pe, ("o", t - 3))
                for b in range(NB):
                    mm = pe.transpose(psum[t % 3][:, 128 * b:128 * b + tn], ug[0:tn, t, 128 * b:128 * b + 128],
                                      ident[0:tn, 0:tn])
                pe_g.done(mm, ("turned", t))
            act_g.wait(pe, ("o", 4))

            units_of("q")
            pe.wait_ge(mem_loaded, 32)
            for n, (m, g) in enumerate(MG):
                bank = psum[6 + n % 2]
                if n >= 2:
                    dve_x.wait(pe, ("lo", *MG[n - 2]))
                for k in range(4):
                    mm = pe.transpose(bank[:, 128 * k:128 * k + 128], mn[:, m, 512 * g + 128 * k:512 * g + 128 * k + 128],
                                      ident[:, :])
                pe_x.done(mm, ("mem", m, g))
            dve_x.wait(pe, ("lo", 1, 1))
            units_of("wk", "wv")
            act_evac.wait(pe, first_unit["wk"] + 1)
            dve_evac.wait(pe, first_unit["wv"] + 1)
            for m in range(2):
                for x in range(XH):
                    mm = pe.transpose(psum[6 + m][:, 128 * x:128 * x + 128], kn[:, m, 128 * x:128 * x + 128], ident[:, :])
                pe_x.done(mm, f"kt{m}")
            act_x.wait(pe, "kt1")

            def score(t, t0, tn):
                for x in range(XH):
                    mm = pe.matmul(psum[x // 2][0:tn, NM * (x % 2):NM * (x % 2) + NM], qt[:, x, t0:t0 + tn], ktm[:, x, :],
                                   start=True, stop=True)
                pe_x.done(mm, ("score", t))

            for t in range(4):
                if t >= 1:
                    act_x.wait(pe, ("p", t - 1))
                    dve_x.wait(pe, ("max", t - 1))
                score(t, 128 * t, 128)
                dve_x.wait(pe, ("p", t))
                for n in range(8):
                    mm = pe.transpose(psum[2 + n // 4][:, 128 * (n % 4):128 * (n % 4) + 128],
                                      prob[:, n // 2, 128 * (n % 2):128 * (n % 2) + 128], ident[:, :])
                pe_x.done(mm, ("turned", t))
                act_x.wait(pe, ("turned", t))
                dve_x.wait(pe, ("turned", t))
                for x in range(XH):
                    for m in range(2):
                        mm = pe.matmul(psum[4][:, 128 * x:128 * x + 128], vn[:, m, 128 * x:128 * x + 128],
                                       prt[:, 2 * x + m, :], start=(m == 0), stop=(m == 1))
                pe_x.done(mm, ("o", t))
            act_x.wait(pe, ("o", 3))
            dve_x.wait(pe, "qm")
            for b in range(DB):
                pe.wait_ge(kv_loaded[b % 4], 16 * (b // 4 + 1))
                if b >= 1:
                    act_x.wait(pe, ("skt", b - 1))
                    dve_x.wait(pe, ("skt", b - 1))
                for x in range(XH):
                    for m in range(2):
                        mm = pe.transpose(psum[6 + x // 2][:, NM * (x % 2) + 128 * m:NM * (x % 2) + 128 * m + 128],
                                          kvs[:, b % 4, m, 128 * x:128 * x + 128], ident[:, :])
                pe_x.done(mm, ("skt", b))
                act_x.wait(pe, ("skt", b))
                dve_x.wait(pe, ("skt", b))
                for x in range(XH):
                    mm = pe.matmul(psum[x // 2][0:NS, NM * (x % 2):NM * (x % 2) + NM], qm[:, x, NS * b:NS * b + NS],
                                   ktm[:, x, :], start=(b == 0 and x % 2 == 0), stop=(b == DB - 1), skip_group_check=True)
            pe_x.done(mm, "sscore")
            dve_x.wait(pe, "sp")
            for n in range(8):
                mm = pe.transpose(psum[2][:, NS * n:NS * n + NS], prob[0:NS, n // 2, 128 * (n % 2):128 * (n % 2) + 128],
                                  ident[0:NS, 0:NS])
            pe_x.done(mm, "sturned")
            act_x.wait(pe, "sturned")
            for b in range(DB):
                pe.wait_ge(kv_loaded[b % 4], 16 * (b // 4 + 3))
                for x in range(XH):
                    for m in range(2):
                        mm = pe.matmul(psum[4][:, NS * x + DS * b:NS * x + DS * b + DS], kvs[:, b % 4, m, 128 * x:128 * x + 128],
                                       prt[:, 2 * x + m, DS * b:DS * b + DS], start=(m == 0), stop=(m == 1))
                pe_v.done(mm, ("v", b))
            act_x.wait(pe, "so")

            dve_m.wait(pe, ("ol", 2))
            units_of("merge")
            dve_m.wait(pe, "ml1")
            units_of("out")
            moe_pe(pe)

        def split_plan():
            done = [0]

            def upto(n, split):
                while done[0] < n:
                    split(done[0])
                    done[0] += 1
            return upto

        def unit_raw(u):
            _, _, j, c0, c1, tiles = units[u]
            width = chunks[j][2]
            return ring[:, j % 2, 0:tiles * width].rearrange("p (k n) -> p k n", n=width)[:, :, c0:c1]

        def unit_part(part, u):
            _, _, _, c0, c1, tiles = units[u]
            return part[:, u % 3, 0:tiles * (c1 - c0)].rearrange("p (k n) -> p k n", n=c1 - c0)

        def chunk_count(j):
            return sum(16 * (2 if chunks[n][0] == "merge" else 1) for n in range(j % 2, j + 1, 2))

        def heads3(ap):
            return ap.rearrange("p (h n) -> p h n", n=64)

        @block.scalar
        def _(act):
            seq = Sequence(act, act_seq)
            upto = split_plan()

            def split(u):
                j = units[u][2]
                act.wait_ge(slot_loaded[j % 2], chunk_count(j))
                if u >= 3:
                    act.wait_ge(unit_used, u - 2)
                act.activation(unit_part(wh, u), unit_raw(u), ACT.Copy).then_inc(hi_ready, 1)

            pe_n1.wait(act, "par")
            act_n1.done(act.activation(par[:, 0:P_OK], psum[7][:, 0:P_OK], ACT.Copy), "par")
            act_n1.done(act.activation(bs_t[:, :], psum[7][:, 64:64 + GG], ACT.Copy), "bs")
            act.wait_ge(x_loaded, 16 * 5)
            dve_n1.wait(act, "clear")
            for t, (_, tn) in enumerate(TILES):
                if t >= 1:
                    act_n1.wait(act, ("sq", t - 1))
                act_n1.done(act.activation(xq[0:tn, :], x_sb[0:tn, t, :], ACT.Square,
                                           accum_out=ssq[0:tn, t:t + 1]), ("sq", t))
            dve_n1.wait(act, "ms")
            act_n1.done(act.activation(rstd[:, 0:5], ssq[:, 0:5], ACT.Sqrt), "root")
            for n, (t, g) in enumerate(TG):
                t0, tn = TILES[t]
                pe_n1.wait(act, ("turned", t, g))
                act_n1.done(act.activation(xnh[:, 4 * g:4 * g + 4, t0:t0 + tn],
                                           psum[n % 7][:, :].rearrange("p (k n) -> p k n", n=128)[:, :, 0:tn],
                                           ACT.Copy), ("hi", t, g))

            for u in range(RWKV_UNITS):
                upto(min(u + 3, RWKV_UNITS), split)
                act.wait_ge(unit_used, u + 1)
                act_evac.done(act.activation(pt[:, 2 * u, 1:SEQ + 1], psum[3 * (u % 2)][:, :], ACT.Copy), u)
            for n in range(4):
                pe_r.wait(act, f"shift_out{n}")
                w_ = min(512, RW - 512 * n)
                act_r.done(act.activation(sho[:, 512 * n:512 * n + w_], psum[n][0:9, 0:w_], ACT.Copy), ("row", n))
            for b in range(RB):
                dve_r.wait(act, ("mixed", b))
                act_r.done(act.activation(pt[:, b, 0:NT], mix[b % 2][:, :], ACT.Copy), ("pt", b))
            act_r.wait(act, ("pt", RB - 1))
            act_r.done(act.activation(wa[0:64, :], pt[0:64, 12, 0:NT], ACT.Tanh), "tanh")
            act_r.done(act.activation(wa[64:128, :], pt[64:128, 12, 0:NT], ACT.Copy), "ad")
            act_r.done(act.activation(pt[:, 13, 0:NT], pt[:, 13, 0:NT], ACT.Sigmoid), "gd")
            for b in range(NB):
                for w, p, dst, c in (("z", 0, sig, P_W0), ("a", 64, aa, P_A0)):
                    n = 4 + 2 * (b % 2) + p // 64
                    pe_r.wait(act, (w, b))
                    if b == 0:
                        act.wait_ge(stored, 32)
                    act.activation(dst[:, b, 0:SEQ], psum[n][:, :], ACT.Sigmoid, bias=par[:, c + b:c + b + 1])
                    act_r.done(act.activation(dst[:, b, SEQ:NT], psum[n - 4][:, 0:NS], ACT.Sigmoid,
                                              bias=par[:, c + b:c + b + 1]), (w, b))
            for b in range(NB):
                dve_r.wait(act, ("kk", b))
                act_r.done(act.activation(o_gm[:, b, :], o_rw[:, b, :], ACT.Square), ("sq", b))
            dve_r.wait(act, ("cut", NB - 1))
            act_r.done(act.activation(o_gm[:, :, :], o_gm[:, :, :], ACT.Sqrt), "root")
            for b in range(NB):
                dve_r.wait(act, ("sum", b))
                if b >= 1:
                    dve_r.wait(act, ("done", b - 1))
                act_r.done(act.activation(e1[:, :], tmp1[:, :], ACT.Exp, scale=-DECAY), ("e1", b))
                dve_r.wait(act, ("less", b))
                act_r.done(act.activation(tmp2[:, :], tmp2[:, :], ACT.Exp, scale=-DECAY), ("e2", b))
                act_r.done(act.activation(tmp1[:, :], tmp1[:, :], ACT.Exp, scale=DECAY), ("e3", b))
            dve_r.wait(act, "bonus")
            dve_r.wait(act, ("done", NB - 1))

            def block_start(i, act_t, cols, rcols, sg):
                act.activation(ar[:, :, 0, :], o_rw[:, :, cols], ACT.Copy)
                act_t.done(act.activation(ar[:, :, 1, :], rcols, ACT.Copy), "ar")
                act.activation(bc[:, :, :], o_gm[:, :, cols], ACT.Copy)
                act_t.done(act.activation(sgc[:, :], sg, ACT.Copy), "rest")

            def block_middle(i, act_t, pe_t, levels):
                pe_t.wait(act, "turn", i)
                act.activation(vt[:, :, :], heads3(psum[3][:, 0:256]), ACT.Copy)
                act.activation(bt[:, :, :], heads3(psum[3][:, 256:512]), ACT.Copy)
                act.activation(kt[:, :, :], heads3(psum[4][:, 0:256]), ACT.Copy)
                act_t.done(act.activation(gt[:, :, :], heads3(psum[4][:, 256:512]), ACT.Copy), "turned")
                for n in levels[:-1]:
                    pe_t.wait(act, ("level", n), i)
                    act_t.done(act.activation(pm[:, :, :], heads3(psum[5][:, 0:256]), ACT.Copy), ("p", n))

            with act.Fori(0, NC) as i:
                await_round(act, blocks_done, i + 1)
                block_start(i, act_b, bass.ds(i * C, C), pt[:, 0:NB, bass.ds(i * C, C)], pt[:, 13, bass.ds(i * C, C)])
                block_middle(i, act_b, pe_b, LEVELS)
                pe_b.wait(act, "x", i)
                act_b.done(act.activation(xt[:, :, :], heads3(psum[5][:, 0:256]), ACT.Copy), "x")
                pe_b.wait(act, "u", i)
                act_b.done(act.activation(ut[:, :, :], heads3(psum[6][:, 0:256]), ACT.Copy), "u")
                pe_b.wait(act, "y", i)
                act_b.done(act.activation(yt[:, :, :], heads3(psum[7][:, 0:256]), ACT.Copy), "y")
                dve_b.wait(act, "centred", i)
                act_b.done(act.activation(ysq[:, :, :], yt[:, :, :], ACT.Square), "sq")
                dve_b.wait(act, "var", i)
                act_b.done(act.activation(mom[:, 2, :], mom[:, 1, :], ACT.Sqrt), "root")
                pe_b.wait(act, "out", i)
                act.activation(o_rw[:, :, bass.ds(i * C, C)], heads3(psum[7][:, 256:512]), ACT.Copy).then_inc(blocks_done, 1)

            pe_s.wait(act, "sfin")
            act_s.done(act.activation(st[:, :, :], heads3(psum[7][:, 0:256]), ACT.Copy), "sfin")
            for b in range(NB):
                pe_s.wait(act, ("s0", b))
                act_s.done(act.activation(s0t[:, b, :, :], heads3(psum[1 + b][:, :]), ACT.Copy), ("s0", b))
            block_start(0, act_s, slice(SEQ, NT), pt[:, 0:NB, SEQ:NT], pt[:, 13, SEQ:NT])
            block_middle(0, act_s, pe_s, LEVELS_S)
            pe_s.wait(act, "u")
            act_s.done(act.activation(ut[:, :, :], heads3(psum[6][:, 0:256]), ACT.Copy), "u")
            dve_s.wait(act, "centred")
            act_s.done(act.activation(ysq[:, :, :], yt[:, :, :], ACT.Square), "sq")
            dve_s.wait(act, "var")
            act_s.done(act.activation(mom[:, 2, :], mom[:, 1, :], ACT.Sqrt), "root")
            for b in range(NB):
                pe_s.wait(act, ("sb", b))
                act_s.done(act.activation(sout[:, :, b, :], heads3(psum[1 + b][:, :]), ACT.Copy), ("sb", b))
            pe_s.wait(act, "out")
            act_s.done(act.activation(o_rw[:, :, SEQ:NT], heads3(psum[7][:, 256:512]), ACT.Copy), "out")

            for u in range(first_unit["u"], first_unit["v"] + 2):
                upto(u + 3, split)
                act.wait_ge(unit_used, u + 1)
                if u == first_unit["u"]:
                    act.wait_ge(stored, 16 * (3 + NB))
                _, n, _, c0, c1, _ = units[u]
                dst = ug if kinds[u] == "u" else vg
                for m in range(2):
                    act.activation(dst[:, 2 * m:2 * m + 2, c0:c1], psum[3 * (u % 2) + m][:, :].rearrange("p (t n) -> p t n", n=256),
                                   ACT.Gelu_apprx_tanh)
                act_evac.done(act.activation(dst[0:NS, 4, c0:c1], psum[3 * (u % 2) + 2][0:NS, 0:256],
                                             ACT.Gelu_apprx_tanh), u)
            for n in range(2):
                pe_g.wait(act, f"w{n}")
                act_g.done(act.activation(wt[:, 4 * n:4 * n + 4, :], psum[n][:, :].rearrange("p (g n) -> p g n", n=128),
                                          ACT.Copy), f"w{n}")
            pe_g.wait(act, "ws")
            act_g.done(act.activation(wst[:, :, :], psum[2][0:NS, :].rearrange("p (g n) -> p g n", n=NS), ACT.Copy), "ws")
            dve_g.wait(act, "var")
            act_g.done(act.activation(mv[:, :, 1], mv[:, :, 1], ACT.Sqrt), "root")
            for t, (t0, tn) in enumerate(TILES):
                pe_g.wait(act, ("turned", t))
                act_g.done(act.activation(o_gm[:, :, t0:t0 + tn],
                                          psum[t % 3][:, :].rearrange("p (b n) -> p b n", n=128)[:, :, 0:tn], ACT.Copy), ("o", t))

            for u in range(first_unit["q"], first_unit["q"] + 2):
                upto(u + 3, split)
                act.wait_ge(unit_used, u + 1)
                n = units[u][1]
                act_evac.done(act.activation(qt[:, 2 * n, 0:SEQ], psum[3 * (u % 2)][:, :], ACT.Copy), u)
            for n, (m, g) in enumerate(MG):
                pe_x.wait(act, ("mem", m, g))
                act_x.done(act.activation(mth[:, 4 * g:4 * g + 4, 128 * m:128 * m + 128],
                                          psum[6 + n % 2][:, :].rearrange("p (k n) -> p k n", n=128), ACT.Copy), ("hi", m, g))
            for u in range(first_unit["wk"], first_unit["wv"] + 2):
                upto(min(u + 3, len(units)), split)
                if kinds[u] == "wk":
                    act.wait_ge(unit_used, u + 1)
                    act_evac.done(act.activation(kn[:, :, units[u][3]:units[u][4]],
                                                 psum[3 * (u % 2)][:, :].rearrange("p (m n) -> p m n", n=256), ACT.Copy), u)
            for m in range(2):
                pe_x.wait(act, f"kt{m}")
                act_x.done(act.activation(ktm[:, :, 128 * m:128 * m + 128],
                                          psum[6 + m][:, :].rearrange("p (x n) -> p x n", n=128), ACT.Copy), f"kt{m}")

            def exps(name, tn):
                dve_x.wait(act, ("max", name) if name is not None else "smax")
                for x in range(XH):
                    e = act.activation(prob[0:tn, x, :], psum[x // 2][0:tn, NM * (x % 2):NM * (x % 2) + NM], ACT.Exp,
                                       bias=smx[0:tn, 1, x:x + 1], scale=128 ** -0.5, accum_out=smx[0:tn, 2, x:x + 1])
                act_x.done(e, ("p", name) if name is not None else "sp")

            for t in range(4):
                exps(t, 128)
                pe_x.wait(act, ("turned", t))
                act_x.done(act.activation(prt[:, 0:4, :], psum[2][:, :].rearrange("p (n t) -> p n t", t=128), ACT.Copy),
                           ("turned", t))
                pe_x.wait(act, ("o", t))
                act_x.done(act.activation(o_xa[:, :, 128 * t:128 * t + 128],
                                          psum[4][:, :].rearrange("p (x t) -> p x t", t=128), ACT.Copy), ("o", t))
            for b in range(DB):
                pe_x.wait(act, ("skt", b))
                act_x.done(act.activation(ktm[:, 0:2, :], psum[6][:, :].rearrange("p (x n) -> p x n", n=NM), ACT.Copy),
                           ("skt", b))
            exps(None, NS)
            pe_x.wait(act, "sturned")
            act_x.done(act.activation(prt[:, :, 0:NS], psum[2][:, :].rearrange("p (n t) -> p n t", t=NS), ACT.Copy), "sturned")
            pe_v.wait(act, ("v", DB - 1))
            act_x.done(act.activation(o_xa[:, :, SEQ:NT], psum[4][:, 0:XH * NS].rearrange("p (x t) -> p x t", t=NS),
                                      ACT.Copy), "so")
            act_x.wait(act, "so")
            for n, o in enumerate((o_gm, o_rw, o_xa)):
                act_m.done(act.activation(oh[:, NB * n:NB * n + NB, :], o[:, :, :], ACT.Copy), ("oh", n))

            for u in range(first_unit["merge"], first_unit["out"]):
                upto(min(u + 3, len(units)), split)
                act.wait_ge(unit_used, u + 1)
                n = units[u][1]
                b, d = (n // 2) % 3, 2 * (n // 6) + n % 2
                bias = par[:, P_GB + KD * b + d:P_GB + KD * b + d + 1]
                if n >= 2:
                    dve_evac.wait(act, u - 2)
                act.activation(gate[n % 2][:, 0:SEQ], psum[3 * (u % 2)][:, :], ACT.Sigmoid, bias=bias)
                act_evac.done(act.activation(gate[n % 2][:, SEQ:NT], psum[3 * (u % 2) + 2][:, 0:NS], ACT.Sigmoid, bias=bias), u)
            dve_evac.wait(act, first_unit["out"] - 1)
            act.wait_ge(unit_used, first_unit["out"])
            for n in range(2):
                act_m.done(act.activation(mh[:, 4 * n:4 * n + 4, :], mt[:, 4 * n:4 * n + 4, :], ACT.Copy), f"mh{n}")
            for u in range(first_unit["out"], len(units)):
                upto(min(u + 3, len(units)), split)
            moe_act(act, seq)

        @block.vector
        def _(dve):
            seq = Sequence(dve, dve_seq)
            upto = split_plan()

            def split(u):
                dve.wait_ge(hi_ready, u + 1)
                dve.tensor_tensor(unit_part(wl, u), unit_raw(u), unit_part(wh, u).bitcast(F32), ALU.subtract)\
                   .then_inc(lo_ready, 1)

            dve_n1.done(dve.memset(ssq[:, :], float(D)), "clear")
            act_n1.wait(dve, ("sq", 4))
            dve_n1.wait(dve, "clear")
            dve_n1.done(dve.tensor_scalar(ssq[:, 0:5], ssq[:, 0:5], 1.0 / D, RMS_EPS, ALU.mult, ALU.add), "ms")
            act_n1.wait(dve, "root")
            seq(dve.reciprocal(rstd[:, 0:5], rstd[:, 0:5]))
            dve.wait_ge(g1_loaded, 16)
            for t, (_, tn) in enumerate(TILES):
                dve_n1.done(dve.scalar_tensor_tensor(x_sb[0:tn, t, :], x_sb[0:tn, t, :], rstd[0:tn, t:t + 1], g1b[0:tn, :],
                                                     ALU.mult, ALU.mult), ("xn", t))
            act_n1.wait(dve, "par")
            dve_n1.done(dve.tensor_scalar(par[:, P_OK:P_END], par[:, P_KA:P_KA + 4], -1.0, 1.0, ALU.mult, ALU.add), "ok")
            for n, (t, g) in enumerate(TG):
                t0, tn = TILES[t]
                act_n1.wait(dve, ("hi", t, g))
                dve_n1.done(dve.tensor_tensor(xnl[:, 4 * g:4 * g + 4, t0:t0 + tn],
                                              psum[n % 7][:, :].rearrange("p (k n) -> p k n", n=128)[:, :, 0:tn],
                                              xnh[:, 4 * g:4 * g + 4, t0:t0 + tn].bitcast(F32), ALU.subtract), ("lo", t, g))

            samples = lambda b: pt[:, b, SEQ + 1:585].rearrange("p (s t) -> p s t", t=DS + 1)
            dve_n1.wait(dve, ("lo", 4, 1))
            seq(dve.memset(pt[:, :, 0:1], 0.0))
            pe_r.wait(dve, "shift_in")
            for b in range(RB):
                last = dve.tensor_copy(samples(b)[:, :, 0], psum[6][:, DB * b:DB * b + DB])
            dve_r.done(last, "prev")
            for u in range(RWKV_UNITS):
                upto(min(u + 3, RWKV_UNITS), split)
                dve.wait_ge(unit_used, u + 1)
                banks = psum[3 * (u % 2):3 * (u % 2) + 3]
                dve.tensor_copy(pt[:, 2 * u + 1, 1:SEQ + 1], banks[1][:, :])
                for m in range(2):
                    last = dve.tensor_copy(samples(2 * u + m)[:, :, 1:DS + 1],
                                           banks[2][:, NS * m:NS * m + NS].rearrange("p (s t) -> p s t", t=DS))
                dve_evac.done(last, u)
            dve_evac.wait(dve, RWKV_UNITS - 1)
            dve_r.wait(dve, "prev")
            pe_r.wait(dve, "shift_out3")
            act_evac.wait(dve, RWKV_UNITS - 1)
            for b in range(RB):
                m = mix[b % 2]
                if b >= 2:
                    act_r.wait(dve, ("pt", b - 2))
                m_s = m[:, SEQ:NT].rearrange("p (s t) -> p s t", t=DS)
                dve.tensor_tensor(m[:, 0:SEQ], pt[:, b, 0:SEQ], pt[:, b, 1:SEQ + 1], ALU.subtract)
                seq(dve.tensor_tensor(m_s, samples(b)[:, :, 0:DS], samples(b)[:, :, 1:DS + 1], ALU.subtract))
                mu = par[:, P_MU + b:P_MU + b + 1]
                dve.scalar_tensor_tensor(m[:, 0:SEQ], m[:, 0:SEQ], mu, pt[:, b, 1:SEQ + 1], ALU.mult, ALU.add)
                dve_r.done(dve.scalar_tensor_tensor(m_s, m_s, mu, samples(b)[:, :, 1:DS + 1], ALU.mult, ALU.add), ("mixed", b))
            for b in range(NB):
                act_r.wait(dve, ("pt", NB + b))
                dve_r.done(dve.tensor_scalar(o_rw[:, b, :], pt[:, NB + b, 0:NT], par[:, P_KK + b:P_KK + b + 1], None, ALU.mult),
                           ("kk", b))
            for b in range(NB):
                pe_r.wait(dve, ("heads", b))
                n = 4 + 2 * (b % 2)
                dve.tensor_scalar(o_gm[:, b, 0:SEQ], psum[n][:, :], 1e-24, None, ALU.max)
                dve_r.done(dve.tensor_scalar(o_gm[:, b, SEQ:NT], psum[n + 1][:, 0:NS], 1e-24, None, ALU.max), ("cut", b))
            act_r.wait(dve, "root")
            seq(dve.reciprocal(o_gm[:, :, :], o_gm[:, :, :]))
            dve_r.done(dve.tensor_tensor(o_rw[:, :, :], o_rw[:, :, :], o_gm[:, :, :], ALU.mult), "unit")
            dve_r.wait(dve, "unit")
            for b in range(NB):
                r_, k_ = pt[:, b, 0:NT], pt[:, NB + b, 0:NT]
                if b >= 1:
                    dve_r.wait(dve, ("done", b - 1))
                dve_r.done(dve.tensor_tensor_scan(tmp1[:, :], restart[:, :], sig[:, b, :], 0.0, ALU.mult, ALU.add), ("sum", b))
                dve_r.wait(dve, ("sum", b))
                dve_r.done(dve.tensor_tensor(tmp2[:, :], tmp1[:, :], sig[:, b, :], ALU.subtract), ("less", b))
                dve_r.wait(dve, ("less", b))
                seq(dve.tensor_scalar(sig[:, b, :], aa[:, b, :], par[:, P_KA + b:P_KA + b + 1], par[:, P_OK + b:P_OK + b + 1],
                                      ALU.mult, ALU.add))
                seq(dve.tensor_tensor(k_, k_, sig[:, b, :], ALU.mult))
                dve_r.done(dve.scalar_tensor_tensor(sig[:, b, :], r_, par[:, P_RK + b:P_RK + b + 1], k_, ALU.mult, ALU.mult),
                           ("rk", b))
                seq(dve.tensor_tensor(o_gm[:, b, :], o_rw[:, b, :], aa[:, b, :], ALU.mult))
                act_r.wait(dve, ("e3", b))
                dve_r.wait(dve, ("rk", b))
                dve.tensor_copy(wcp[:, b, :], e1[:, C - 1:SEQ:C])
                dve.tensor_copy(wcs[:, b, :], e1[:, SEQ + DS - 1:NT:DS])
                dve.tensor_tensor(r_, r_, e1[:, :], ALU.mult)
                dve.tensor_tensor(k_, k_, tmp1[:, :], ALU.mult)
                dve.tensor_tensor(o_gm[:, b, :], o_gm[:, b, :], tmp1[:, :], ALU.mult)
                dve_r.done(dve.scalar_tensor_tensor(o_rw[:, b, :], o_rw[:, b, :], -1.0, tmp2[:, :], ALU.mult, ALU.mult),
                           ("done", b))
            dve_r.wait(dve, ("done", NB - 1))
            pe_r.wait(dve, ("bonus", NB - 1))
            dve_r.done(dve.tensor_copy(bon[:, :, :], psum[0][:, 0:NB * (NC + 1)].rearrange("p (c b) -> p c b", b=NB)), "bonus")
            dve_r.wait(dve, "bonus")
            dve.memset(mom[:, :, :], 0.0).then_inc(blocks_done, 1)
            dve.memset(st[:, :, :], 0.0).then_inc(state_ready, 1)

            def four(ap):
                return ap.unsqueeze(1).to_broadcast([128, NB, C])

            def over_i(ap):
                return ap.unsqueeze(2).to_broadcast([128, NB, C])

            def masks(i, pe_t, dve_t, levels, m):
                pe_t.wait(dve, "mt", i)
                mt_ = psum[0][:, :].rearrange("p (b x n) -> p b x n", x=2, n=C)
                mk_ = psum[1][:, :].rearrange("p (b x n) -> p b x n", x=2, n=C)
                seq(dve.tensor_tensor(ptt[:, :, 0, :], mt_[:, :, 0, :], four(up_s[:, m, :]), ALU.mult))
                dve.tensor_tensor(rbt[:, :, :], mt_[:, :, 1, :], four(up_i[:, m, :]), ALU.mult)
                dve.tensor_tensor(ptt[:, :, 1, :], ptt[:, :, 0, :], four(i64[:, :]), ALU.add)
                pe_t.wait(dve, "mk", i)
                dve.tensor_tensor(mkt[:, :, :], mk_[:, :, 0, :], four(up_s[:, m, :]), ALU.mult)
                dve.tensor_tensor(rkt[:, :, :], mk_[:, :, 1, :], four(up_i[:, m, :]), ALU.mult)
                pe_t.wait(dve, "m", i)
                dve_t.done(dve.tensor_tensor(pm[:, :, :], heads3(psum[2][:, 0:256]), four(low_s[:, m, :]), ALU.mult), "masked")
                for n in levels:
                    pe_t.wait(dve, ("level", n), i)
                    lv = psum[0][:, :].rearrange("p (b x n) -> p b x n", x=2, n=C)
                    if n != levels[-1]:
                        last = dve.tensor_copy(ptt[:, :, 0, :], lv[:, :, 0, :])
                    if n > 0:
                        dve_t.wait(dve, ("level", n - 1), i)
                        last = dve.tensor_tensor(ptt[:, :, 1, :], ptt[:, :, 1, :], lv[:, :, 1, :], ALU.add)
                    dve_t.done(last, ("level", n))

            def centre():
                seq(dve.tensor_reduce(mom[:, 0, :], yt[:, :, :], AX.X, ALU.add))
                seq(dve.tensor_scalar(mom[:, 0, :], mom[:, 0, :], -1.0 / HD, None, ALU.mult))
                return dve.tensor_tensor(yt[:, :, :], yt[:, :, :], over_i(mom[:, 0, :]), ALU.add)

            def variance():
                seq(dve.tensor_reduce(mom[:, 3, :], ysq[:, :, :], AX.X, ALU.add))
                return dve.tensor_scalar(mom[:, 1, :], mom[:, 3, :], 1.0 / HD, GN_EPS, ALU.mult, ALU.add)

            def finish():
                seq(dve.reciprocal(mom[:, 2, :], mom[:, 2, :]))
                seq(dve.tensor_tensor(yt[:, :, :], yt[:, :, :], over_i(mom[:, 2, :]), ALU.mult))
                seq(dve.tensor_tensor(yt[:, :, :], yt[:, :, :], lnx[:, 0, :, :], ALU.mult))
                seq(dve.tensor_tensor(yt[:, :, :], yt[:, :, :], lnx[:, 1, :, :], ALU.add))
                seq(dve.tensor_tensor(yt[:, :, :], yt[:, :, :], bv[:, :, :], ALU.add))
                return dve.tensor_tensor(yt[:, :, :], yt[:, :, :], gt[:, :, :], ALU.mult)

            with dve.Fori(0, NC) as i:
                seq.enter(i, 10)
                await_round(dve, blocks_done, i + 1)
                dve.tensor_copy(kc[:, :, :], pt[:, NB:2 * NB, bass.ds(i * C, C)])
                dve_b.done(dve.tensor_copy(vc[:, :, :], pt[:, 2 * NB:3 * NB, bass.ds(i * C, C)]), "copied")
                masks(i, pe_b, dve_b, LEVELS, 0)
                pe_b.wait(dve, "s", i)
                seq(dve.tensor_tensor(st[:, :, :], st[:, :, :], heads3(psum[6][:, 0:256]), ALU.add))
                dve.tensor_tensor(st[:, :, :], st[:, :, :], over_i(wcp[:, :, bass.ds(i, 1)].rearrange("p b c -> p (b c)")), ALU.mult).then_inc(state_ready, 1)
                act_b.wait(dve, "y", i)
                dve_b.done(centre(), "centred")
                act_b.wait(dve, "sq", i)
                dve_b.done(variance(), "var")
                act_b.wait(dve, "root", i)
                pool_b.wait(dve, "bonus", i)
                dve_b.done(finish(), "o")
            seq.leave(NC)

            dve.wait_ge(blocks_done, NC + 1)
            dve.tensor_copy(kc[:, :, :], pt[:, NB:2 * NB, SEQ:NT])
            dve_s.done(dve.tensor_copy(vc[:, :, :], pt[:, 2 * NB:3 * NB, SEQ:NT]), "copied")
            masks(0, pe_s, dve_s, LEVELS_S, 1)
            act_s.wait(dve, "rest")
            dve_s.wait(dve, "copied")
            own_ = own[:, :].unsqueeze(2).to_broadcast([128, DB, HD])

            def keep_own(name, dst):
                for b in range(NB):
                    pe_s.wait(dve, (name, b))
                    seq(dve.tensor_tensor(big[b][:, :, :], heads3(psum[1 + b][:, :]), own_, ALU.mult))
                    dve_s.done(dve.tensor_reduce(dst[:, b, :], big[b][:, :, :].rearrange("p s i -> p i s"), AX.X, ALU.add),
                               (name, b))
            keep_own("xs", xt)
            pe_s.wait(dve, "x")
            dve_s.wait(dve, ("xs", NB - 1))
            dve_s.done(dve.tensor_tensor(xt[:, :, :], xt[:, :, :], heads3(psum[5][:, 0:256]), ALU.add), "x")
            keep_own("ys", yt)
            act_s.wait(dve, "u")
            dve_s.wait(dve, ("ys", NB - 1))
            for b in range(NB):
                if b >= 2:
                    pe_s.wait(dve, ("sn", b - 2))
                for n, src in enumerate((ut, vt)):
                    last = dve.tensor_tensor(big[2 * (b % 2) + n][:, :, :], src[:, b, :].unsqueeze(1).to_broadcast([128, DB, HD]),
                                             own_, ALU.mult)
                dve_s.done(last, ("spread", b))
            pe_s.wait(dve, "y")
            seq(dve.tensor_tensor(yt[:, :, :], yt[:, :, :], heads3(psum[7][:, 0:256]), ALU.add))
            dve_s.done(centre(), "centred")
            act_s.wait(dve, "sq")
            dve_s.done(variance(), "var")
            for b in range(NB):
                pe_s.wait(dve, ("sn", b))
                seq(dve.tensor_tensor(s0t[:, b, :, :], s0t[:, b, :, :], heads3(psum[1 + b][:, :]), ALU.add))
                dve_s.done(dve.tensor_tensor(s0t[:, b, :, :], s0t[:, b, :, :],
                                             wcs[:, b, :].unsqueeze(2).to_broadcast([128, DB, HD]), ALU.mult), ("sn", b))
            act_s.wait(dve, "root")
            pool_s.wait(dve, "bonus")
            dve_s.done(finish(), "o")

            for u in range(first_unit["u"], first_unit["v"] + 2):
                upto(u + 3, split)
                dve.wait_ge(unit_used, u + 1)
            act_evac.wait(dve, first_unit["v"] + 1)
            seq(dve.memset(mv[:, :, :], 1.0))
            for t, (_, tn) in enumerate(TILES):
                seq(dve.bn_stats(bst[0:tn, t, :], vg[0:tn, t, :]))
                seq(dve.bn_aggr(mv[0:tn, t, :], bst[0:tn, t, :]))
            dve_g.done(dve.tensor_scalar(mv[:, :, 1], mv[:, :, 1], LN_EPS, None, ALU.add), "var")
            act_g.wait(dve, "root")
            dve.wait_ge(gm_loaded, 16 * (3 + DB))
            seq(dve.reciprocal(mv[:, :, 1], mv[:, :, 1]))
            for t, (_, tn) in enumerate(TILES):
                v_ = vg[0:tn, t, :]
                seq(dve.tensor_scalar(v_, v_, mv[0:tn, t, 0:1], mv[0:tn, t, 1:2], ALU.subtract, ALU.mult))
                seq(dve.tensor_tensor(v_, v_, lng[0:tn, 0, :], ALU.mult))
                dve_g.done(dve.tensor_tensor(v_, v_, lng[0:tn, 1, :], ALU.add), ("vn", t))
            for t, (_, tn) in enumerate(TILES):
                pe_g.wait(dve, ("s", t))
                if t >= 1:
                    dve_g.wait(dve, ("o", t - 1))
                bias = (bs_s if t == 4 else bs_t)[0:tn, :].unsqueeze(2).to_broadcast([tn, GG, HD])
                seq(dve.tensor_tensor(heads3(gtmp[0:tn, :]), heads3(psum[3 + t][0:tn, :]), bias, ALU.add))
                dve_g.done(dve.tensor_tensor(ug[0:tn, t, :], ug[0:tn, t, :], gtmp[0:tn, :], ALU.mult), ("o", t))

            for u in range(first_unit["q"], first_unit["q"] + 2):
                upto(u + 3, split)
                dve.wait_ge(unit_used, u + 1)
                if u == first_unit["q"]:
                    act_g.wait(dve, ("o", 4))
                    dve.wait_ge(stored, 16 * (4 + NB))
                n, banks = units[u][1], psum[3 * (u % 2):3 * (u % 2) + 3]
                dve.tensor_copy(qt[:, 2 * n + 1, 0:SEQ], banks[1][:, :])
                dve_evac.done(dve.tensor_copy(qt[:, 2 * n:2 * n + 2, SEQ:NT],
                                              banks[2][:, 0:2 * NS].rearrange("p (m t) -> p m t", t=NS)), u)
            for n, (m, g) in enumerate(MG):
                act_x.wait(dve, ("hi", m, g))
                cut = (slice(None), slice(4 * g, 4 * g + 4), slice(128 * m, 128 * m + 128))
                dve_x.done(dve.tensor_tensor(mtl[cut], psum[6 + n % 2][:, :].rearrange("p (k n) -> p k n", n=128),
                                             mth[cut].bitcast(F32), ALU.subtract), ("lo", m, g))
            for u in range(first_unit["wk"], first_unit["wv"] + 2):
                upto(min(u + 3, len(units)), split)
                if kinds[u] == "wv":
                    dve.wait_ge(unit_used, u + 1)
                    dve_evac.done(dve.tensor_copy(vn[:, :, units[u][3]:units[u][4]],
                                                  psum[3 * (u % 2)][:, :].rearrange("p (m n) -> p m n", n=256)), u)

            def maxima(tn, name):
                for g in range(2):
                    last = dve.tensor_reduce(smx[0:tn, 0, 2 * g:2 * g + 2],
                                             psum[g][0:tn, :].rearrange("p (x n) -> p x n", n=NM), AX.X, ALU.max)
                seq(last)
                dve_x.done(dve.tensor_scalar(smx[0:tn, 1, :], smx[0:tn, 0, :], -(128 ** -0.5), None, ALU.mult), name)

            def normalise(tn, name):
                seq(dve.reciprocal(smx[0:tn, 3, :], smx[0:tn, 2, :]))
                dve_x.done(dve.tensor_tensor(prob[0:tn, :, :], prob[0:tn, :, :],
                                             smx[0:tn, 3, :].unsqueeze(2).to_broadcast([tn, XH, NM]), ALU.mult), name)

            for t in range(4):
                pe_x.wait(dve, ("score", t))
                maxima(128, ("max", t))
                act_x.wait(dve, ("p", t))
                normalise(128, ("p", t))
                pe_x.wait(dve, ("turned", t))
                dve_x.done(dve.tensor_copy(prt[:, 4:8, :], psum[3][:, :].rearrange("p (n t) -> p n t", t=128)), ("turned", t))
            seq(dve.memset(qm[:, :, :], 0.0))
            for x in range(XH):
                last = dve.tensor_copy(qm[:, x, :].rearrange("p (b n) -> p b n", n=NS + DS)[:, :, 0:DS],
                                       qt[:, x, SEQ:NT].rearrange("p (b n) -> p b n", n=DS))
            dve_x.done(last, "qm")
            for b in range(DB):
                pe_x.wait(dve, ("skt", b))
                dve_x.done(dve.tensor_copy(ktm[:, 2:4, :], psum[7][:, :].rearrange("p (x n) -> p x n", n=NM)), ("skt", b))
            pe_x.wait(dve, "sscore")
            maxima(NS, "smax")
            act_x.wait(dve, "sp")
            normalise(NS, "sp")
            dve_x.done(dve.tensor_copy(smx[0:NS, 0, :], smx[0:NS, 1, :]), "sturned")
            for n, o in enumerate((o_gm, o_rw, o_xa)):
                act_m.wait(dve, ("oh", n))
                dve_m.done(dve.tensor_tensor(ol[:, NB * n:NB * n + NB, :], o[:, :, :], oh[:, NB * n:NB * n + NB, :].bitcast(F32),
                                             ALU.subtract), ("ol", n))

            for u in range(first_unit["merge"], first_unit["out"]):
                upto(min(u + 3, len(units)), split)
                act_evac.wait(dve, u)
                n, banks = units[u][1], psum[3 * (u % 2):3 * (u % 2) + 3]
                b, d = (n // 2) % 3, 2 * (n // 6) + n % 2
                if n == 0:
                    dve_m.wait(dve, ("ol", 2))
                else:
                    dve_evac.wait(dve, u - 1)
                dst = mt[:, d, :] if b == 0 else prod[:, :]
                dve.tensor_tensor(dst[:, 0:SEQ], gate[n % 2][:, 0:SEQ], banks[1][:, :], ALU.mult)
                last = dve.tensor_tensor(dst[:, SEQ:NT], gate[n % 2][:, SEQ:NT], banks[2][:, NS:2 * NS], ALU.mult)
                if b > 0:
                    seq(last)
                    last = dve.tensor_tensor(mt[:, d, :], mt[:, d, :], prod[:, :], ALU.add)
                dve_evac.done(last, u)
            for n in range(2):
                act_m.wait(dve, f"mh{n}")
                dve_m.done(dve.tensor_tensor(ml[:, 4 * n:4 * n + 4, :], mt[:, 4 * n:4 * n + 4, :],
                                             mh[:, 4 * n:4 * n + 4, :].bitcast(F32), ALU.subtract), f"ml{n}")
            for u in range(first_unit["out"], len(units)):
                upto(min(u + 3, len(units)), split)
                dve.wait_ge(unit_used, u + 1)
                dve.wait_ge(x2_loaded, 16 * 5)
                c0 = chunks[units[u][2]][1][1] + units[u][3]
                banks = psum[3 * (u % 2):3 * (u % 2) + 3]
                for m in range(2):
                    hv = h[:, 2 * m:2 * m + 2, c0:c0 + 256]
                    dve.tensor_tensor(hv, hv, banks[m][:, :].rearrange("p (t n) -> p t n", n=256), ALU.add)
                hv = h[0:NS, 4, c0:c0 + 256]
                dve_evac.done(dve.tensor_tensor(hv, hv, banks[2][0:NS, 0:256], ALU.add), u)
            moe_dve(dve, seq)

        @block.gpsimd
        def _(pool):
            seq = Sequence(pool, pool_seq)

            def select(ap, pattern, base, channel, op, fill):
                return seq(pool.affine_select(out=ap, in_=ap, compare_op=op, fill=fill, base=base, pattern=pattern,
                                              channel_multiplier=channel))

            seq(pool.memset(ident[:, :], 0.0))
            select(ident[:, :], [[-1, 128]], 0, 1, ALU.not_equal, 1.0)
            seq(pool.memset(i64[:, :], 0.0))
            for p in (0, 64):
                select(i64[p:p + 64, :], [[-1, 64]], 0, 1, ALU.not_equal, 1.0)
            seq(pool.memset(ones[:, :], 1.0))
            seq(pool.memset(before[:, :], 1.0))
            select(before[:, :], [[1, 128]], 0, -1, ALU.is_gt, 0.0)
            seq(pool.memset(same_head[:, :], 0.0))
            for p in (0, 64):
                seq(pool.memset(same_head[p:p + 64, p:p + 64], 1.0))
            seq(pool.memset(own[:, :], 1.0))
            for p in (0, 64):
                select(own[p:p + 64, :], [[-DS, DB]], 0, 1, ALU.is_ge, 0.0)
                select(own[p:p + 64, :], [[DS, DB]], DS - 1, -1, ALU.is_ge, 0.0)
            for m, sign, op in ((low_s, 1, ALU.is_gt), (up_s, -1, ALU.is_gt), (up_i, -1, ALU.is_ge)):
                seq(pool.memset(m[:, :, :], 1.0))
                for p in (0, 64):
                    select(m[p:p + 64, 0, :], [[-sign, 64]], 0, sign, op, 0.0)
                seq(pool.tensor_tensor(m[:, 1, :].rearrange("p (b s) -> p b s", s=DS), m[:, 0, :].rearrange("p (b s) -> p b s", s=DS),
                                       own[:, :].unsqueeze(2).to_broadcast([128, DB, DS]), ALU.mult))
            seq(pool.memset(restart[:, :], 1.0))
            seq(pool.memset(restart[:, 0:SEQ:C], 0.0))
            pool.memset(restart[:, SEQ:NT:DS], 0.0).then_inc(consts_ready, 1)

            def bonus(src):
                return pool.tensor_tensor(bv[:, :, :], vt[:, :, :], src.unsqueeze(2).to_broadcast([128, NB, C]), ALU.mult)

            dve_r.wait(pool, "bonus")
            with pool.Fori(0, NC) as i:
                act_b.wait(pool, "turned", i)
                pool_b.done(bonus(bon[:, bass.ds(i, 1), :].rearrange("p c b -> p (c b)")), "bonus")
            act_s.wait(pool, "turned")
            pool_s.done(bonus(bon[:, NC, :]), "bonus")

            act_s.wait(pool, "out")
            pool.wait_ge(stored, 16 * (3 + NB))
            pool_g.done(pool.memset(wsn[:, :, :], 0.0), "zero")
            pool.wait_ge(gm_loaded, 16 * (3 + DB))
            seq(pool.affine_select(out=wn[:, :, :], in_=wn[:, :, :], compare_op=ALU.is_ge, fill=0.0, base=0,
                                   pattern=[[0, GG], [-1, CH]], channel_multiplier=1))
            pool.wait_ge(diag_loaded, 16 * DB)
            pool_g.done(pool.affine_select(out=wsn[:, :, :], in_=wsn[:, :, :], compare_op=ALU.is_ge, fill=0.0, base=0,
                                           pattern=[[0, GG], [-1, NS]], channel_multiplier=1), "causal")
            moe_pool(pool, seq)


_INS = ["x_prompt", "x_sample", "state_rwkv_S", "state_rwkv_shift", "cache_mem_k", "cache_mem_v", "mem_prompt",
        "norm1_g", "w_in", "gate_b", "gm_ln_g", "gm_ln_b", "gm_ws", "gm_bs", "rw_mu", "rw_w0", "rw_w2", "rw_a0",
        "rw_a2", "rw_g2", "rw_k_k", "rw_k_a", "rw_r_k", "rw_lnx_g", "rw_lnx_b", "xa_wk", "xa_wv", "w_branch",
        "w_out", "norm2_g", "rg_w", "rg_b", "re_w", "re_b", "e_wg", "e_wu", "e_wd", "final_g"]
_OUTS = [(1, SEQ, D), (DB, DS, D), (1, 1, 2 * NB, HD, HD), (1, 1, RW), (1, 1, NM, XH, 128), (1, 1, NM, XH, 128),
         (1, DB, 2 * NB, HD, HD), (1, DB, RW), (1, DB, DS, W)]


def kernel(**inputs):
    import numpy as _np
    import concourse.bacc as _bacc
    from concourse import mybir as _mybir
    from concourse.bass_utils import run_bass_kernel_spmd as _run

    nc = _bacc.Bacc("TRN2", target_bir_lowering=False, num_devices=1)
    arrays, args = {}, []
    for name in _INS:
        a = _np.ascontiguousarray(inputs[name])
        arrays[f"in_{name}_dram"] = a
        args.append(nc.dram_tensor(f"in_{name}_dram", a.shape, _mybir.dt.from_np(a.dtype), kind="ExternalInput").ap())
    for i, shape in enumerate(_OUTS):
        args.append(nc.dram_tensor(f"out_{i}_dram", shape, _mybir.dt.float32, kind="ExternalOutput").ap())
    build(nc, *args)
    r = _run(nc, [arrays], core_ids=[0])
    return tuple(r.results[0][f"out_{i}_dram"] for i in range(len(_OUTS)))
```
